# Optimizing a Trainium2 kernel written in Bass

```python
import math
import jax, jax.numpy as jnp
from jax import lax
import numpy as np

D_MODEL = 1024
BATCH = 1
SEQ = 1024
DEPTH = 1

CHUNK = 64
LEFT_CHUNKS = 8
BAND_CHUNKS = LEFT_CHUNKS + 1
BAND = BAND_CHUNKS * CHUNK
MAX_REL = 128
N_REL = (CHUNK - 1) + MAX_REL + 1

CONV_WIDTH = D_MODEL // 2
CONV_KERNEL = 31
ATT_HEADS = 8
ATT_HEAD_DIM = 64
ATT_WIDTH = ATT_HEADS * ATT_HEAD_DIM
MEM_LEN = 256
MEM_HEADS = 4
MEM_HEAD_DIM = 128
MEM_WIDTH = MEM_HEADS * MEM_HEAD_DIM
N_BRANCHES = 3
D_FF = 2816
EPS = 1e-6
MASK_VALUE = -1e30

COL_CONV = 2 * CONV_WIDTH
COL_ATT = 3 * ATT_WIDTH
COL_MEM = MEM_WIDTH
COL_GATE = N_BRANCHES * D_MODEL
IN_COLS = COL_CONV + COL_ATT + COL_MEM + COL_GATE

kernel_name = "chunk_causal_hybrid_conformer_block"

def rms_norm(x, g):
    xf = x.astype(jnp.float32)
    y = xf * lax.rsqrt(jnp.mean(xf * xf, axis=-1, keepdims=True) + EPS)
    return (y * g.astype(jnp.float32)).astype(x.dtype)

def layer_norm(x, g, b):
    xf = x.astype(jnp.float32)
    mu = jnp.mean(xf, axis=-1, keepdims=True)
    xc = xf - mu
    y = xc * lax.rsqrt(jnp.mean(xc * xc, axis=-1, keepdims=True) + EPS)
    return (y * g.astype(jnp.float32) + b.astype(jnp.float32)).astype(x.dtype)

def swiglu_ffn(h, w_up, w_down):
    a, b = jnp.split(h @ w_up, 2, axis=-1)
    return (jax.nn.silu(a) * b) @ w_down

def conv_module(u, dw_w, dw_b, ln_g, ln_b, w_pw):
    a, g = jnp.split(u, 2, axis=-1)
    v = a * jax.nn.sigmoid(g)
    v = jnp.pad(v, ((0, 0), (CONV_KERNEL - 1, 0), (0, 0)))
    v = lax.conv_general_dilated(
        v, dw_w[:, None, :].astype(v.dtype), window_strides=(1,), padding="VALID",
        dimension_numbers=("NWC", "WIO", "NWC"), feature_group_count=CONV_WIDTH)
    v = v + dw_b
    v = jax.nn.silu(layer_norm(v, ln_g, ln_b))
    return v @ w_pw

def chunked_attention(q, k, v, rel_bias, w_o):
    B, S, _ = q.shape
    nc = S // CHUNK
    q = q.reshape(B, nc, CHUNK, ATT_HEADS, ATT_HEAD_DIM)
    pad = ((0, 0), (LEFT_CHUNKS * CHUNK, 0), (0, 0))
    kc = jnp.pad(k, pad).reshape(B, nc + LEFT_CHUNKS, CHUNK, ATT_HEADS, ATT_HEAD_DIM)
    vc = jnp.pad(v, pad).reshape(B, nc + LEFT_CHUNKS, CHUNK, ATT_HEADS, ATT_HEAD_DIM)
    band_idx = jnp.arange(nc)[:, None] + jnp.arange(BAND_CHUNKS)[None, :]
    kb = kc[:, band_idx].reshape(B, nc, BAND, ATT_HEADS, ATT_HEAD_DIM)
    vb = vc[:, band_idx].reshape(B, nc, BAND, ATT_HEADS, ATT_HEAD_DIM)
    scores = jnp.einsum("bcqhd,bckhd->bhcqk", q, kb,
                        preferred_element_type=jnp.float32) * (ATT_HEAD_DIM ** -0.5)
    dist = (LEFT_CHUNKS * CHUNK + jnp.arange(CHUNK)[:, None]) - jnp.arange(BAND)[None, :]
    rel_idx = jnp.clip(dist, -(CHUNK - 1), MAX_REL) + (CHUNK - 1)
    bias = rel_bias.astype(jnp.float32)[:, rel_idx]
    key_pos = jnp.arange(nc)[:, None] * CHUNK + jnp.arange(BAND)[None, :] - LEFT_CHUNKS * CHUNK
    valid = (key_pos >= 0)[None, None, :, None, :]
    scores = jnp.where(valid, scores + bias[None, :, None], MASK_VALUE)
    p = jax.nn.softmax(scores, axis=-1).astype(v.dtype)
    o = jnp.einsum("bhcqk,bckhd->bcqhd", p, vb).reshape(B, S, ATT_WIDTH)
    return o @ w_o

def memory_attention(mq, mem_h, w_kv, w_o):
    B, S, _ = mq.shape
    mk, mv = jnp.split(mem_h @ w_kv, 2, axis=-1)
    mq = mq.reshape(B, S, MEM_HEADS, MEM_HEAD_DIM)
    mk = mk.reshape(B, -1, MEM_HEADS, MEM_HEAD_DIM)
    mv = mv.reshape(B, -1, MEM_HEADS, MEM_HEAD_DIM)
    scores = jnp.einsum("bshd,bmhd->bhsm", mq, mk,
                        preferred_element_type=jnp.float32) * (MEM_HEAD_DIM ** -0.5)
    p = jax.nn.softmax(scores, axis=-1).astype(mv.dtype)
    o = jnp.einsum("bhsm,bmhd->bshd", p, mv).reshape(B, S, MEM_WIDTH)
    return o @ w_o

def setup_inputs(seed: int = 0) -> dict:
    key = jax.random.key(seed)
    ks = jax.random.split(key, 24)
    L = DEPTH

    def nrm(k, shape, scale):
        return jax.random.normal(k, shape, jnp.float32) * scale

    def gain(k, shape):
        return 1.0 + nrm(k, shape, 0.05)

    return {
        "x": nrm(ks[0], (BATCH, SEQ, D_MODEL), 1.0),
        "mem": nrm(ks[1], (BATCH, MEM_LEN, D_MODEL), 1.0),
        "ffn1_norm": gain(ks[2], (L, D_MODEL)),
        "ffn1_w_up": nrm(ks[3], (L, D_MODEL, 2 * D_FF), D_MODEL ** -0.5),
        "ffn1_w_down": nrm(ks[4], (L, D_FF, D_MODEL), D_FF ** -0.5),
        "mix_norm": gain(ks[5], (L, D_MODEL)),
        "mem_norm": gain(ks[6], (L, D_MODEL)),
        "w_in": nrm(ks[7], (L, D_MODEL, IN_COLS), D_MODEL ** -0.5),
        "b_gate": nrm(ks[8], (L, N_BRANCHES * D_MODEL), 0.1),
        "conv_dw_w": nrm(ks[9], (L, CONV_KERNEL, CONV_WIDTH), CONV_KERNEL ** -0.5),
        "conv_dw_b": nrm(ks[10], (L, CONV_WIDTH), 0.02),
        "conv_ln_g": gain(ks[11], (L, CONV_WIDTH)),
        "conv_ln_b": nrm(ks[12], (L, CONV_WIDTH), 0.02),
        "conv_w_pw": nrm(ks[13], (L, CONV_WIDTH, D_MODEL), CONV_WIDTH ** -0.5),
        "att_rel_bias": nrm(ks[14], (L, ATT_HEADS, N_REL), 0.5),
        "att_w_o": nrm(ks[15], (L, ATT_WIDTH, D_MODEL), ATT_WIDTH ** -0.5),
        "mem_w_kv": nrm(ks[16], (L, D_MODEL, 2 * MEM_WIDTH), D_MODEL ** -0.5),
        "mem_w_o": nrm(ks[17], (L, MEM_WIDTH, D_MODEL), MEM_WIDTH ** -0.5),
        "w_out": nrm(ks[18], (L, D_MODEL, D_MODEL), D_MODEL ** -0.5),
        "ffn2_norm": gain(ks[19], (L, D_MODEL)),
        "ffn2_w_up": nrm(ks[20], (L, D_MODEL, 2 * D_FF), D_MODEL ** -0.5),
        "ffn2_w_down": nrm(ks[21], (L, D_FF, D_MODEL), D_FF ** -0.5),
        "final_norm": gain(ks[22], (D_MODEL,)),
    }

def reference(x, mem, ffn1_norm, ffn1_w_up, ffn1_w_down, mix_norm, mem_norm, w_in,
              b_gate, conv_dw_w, conv_dw_b, conv_ln_g, conv_ln_b, conv_w_pw,
              att_rel_bias, att_w_o, mem_w_kv, mem_w_o, w_out, ffn2_norm,
              ffn2_w_up, ffn2_w_down, final_norm):
    B, S, _ = x.shape
    for l in range(DEPTH):
        x = x + 0.5 * swiglu_ffn(rms_norm(x, ffn1_norm[l]), ffn1_w_up[l], ffn1_w_down[l])

        h = rms_norm(x, mix_norm[l])
        proj = h @ w_in[l]
        u_conv, qkv, mq, g_logits = jnp.split(
            proj, [COL_CONV, COL_CONV + COL_ATT, COL_CONV + COL_ATT + COL_MEM], axis=-1)
        q, k, v = jnp.split(qkv, 3, axis=-1)

        y_conv = conv_module(u_conv, conv_dw_w[l], conv_dw_b[l], conv_ln_g[l],
                             conv_ln_b[l], conv_w_pw[l])
        y_att = chunked_attention(q, k, v, att_rel_bias[l], att_w_o[l])
        y_mem = memory_attention(mq, rms_norm(mem, mem_norm[l]), mem_w_kv[l], mem_w_o[l])

        gates = jax.nn.sigmoid(g_logits + b_gate[l]).reshape(B, S, N_BRANCHES, D_MODEL)
        y = gates[:, :, 0] * y_conv + gates[:, :, 1] * y_att + gates[:, :, 2] * y_mem
        x = x + y @ w_out[l]

        x = x + 0.5 * swiglu_ffn(rms_norm(x, ffn2_norm[l]), ffn2_w_up[l], ffn2_w_down[l])
    return rms_norm(x, final_norm)


_drawn_inputs = setup_inputs


def setup_inputs(seed=0):
    import zlib

    import numpy as np

    out = dict(_drawn_inputs(seed))
    spreads = {}
    factors = {'mix_norm': 2.825,
     'mem_norm': 8.0,
     'b_gate': 4.669,
     'conv_dw_b': 15.666,
     'conv_ln_g': 10.698,
     'conv_ln_b': 29.339,
     'ffn2_norm': 3.012}
    for name, (base, spread) in spreads.items():
        noise = np.random.default_rng([zlib.crc32(name.encode()), seed]).standard_normal(out[name].shape)
        drawn = base * np.exp(spread * noise) if base else spread * noise
        out[name] = __import__('jax').numpy.asarray(drawn.astype(out[name].dtype))
    for name, factor in factors.items():
        out[name] = (out[name] * factor).astype(out[name].dtype)
    return out
```

```python
from contextlib import ExitStack

import concourse.bass as bass
from concourse import mybir

F32 = mybir.dt.float32
F32R = mybir.dt.float32r
ALU = mybir.AluOpType
ACT = mybir.ActivationFunctionType
AX = mybir.AxisListType

P = 128
T = 1024
HALF = 512
D = 1024
KT = D // P
D_FF = 2816
PAIRS = D_FF // (2 * P)
CONV = 512
CT = CONV // P
TAPS = 31
PAD = TAPS - 1
MEM = 256
MT = MEM // P
HEADS = 8
DH = 64
REL = 192
BANDK = 640
EXT = 768
MH = 4
EPS = 1e-6
NEG = -1e30
BIG = 3.0e38

U_FFN1 = 0
U_KV = U_FFN1 + 6 * PAIRS
U_QKV = U_KV + 8
U_CONV = U_QKV + 3 * 4
U_ATT = U_CONV + 2 * CT
U_MQ = U_ATT + 12
U_MEMO = U_MQ + MH
U_CONVO = U_MEMO + 12
U_OUT = U_CONVO + 12
U_FFN2 = U_OUT + KT
UNITS = U_FFN2 + 6 * PAIRS

C_FFN1, C_MIX, C_MEM, C_FFN2, C_FINAL = 0, 8, 16, 24, 32
C_GATE = 40
C_DW = C_GATE + 24
C_DWB = C_DW + CT * TAPS
C_LNG = C_DWB + CT
C_LNB = C_LNG + CT
N_PAR = C_LNB + CT


def program(nc, x_in, mem_in, weights, params_in, rel_in, y_out):
    rel_ext = nc.dram_tensor("rel_ext", (HEADS, EXT), F32, kind="Internal")
    bias_rows = nc.dram_tensor("bias_rows", (HEADS, P, BANDK), F32, kind="Internal").ap()
    x_spill = nc.dram_tensor("x_spill", (KT, P, T), F32, kind="Internal").ap()

    with ExitStack() as ctx:
        def sem(name):
            return ctx.enter_context(nc.semaphore(name))

        at = [(nc.sbuf_base + 31) // 32 * 32]

        def place(name, shape, dt, offset):
            return nc.alloc_sbuf_tensor_at(name, shape, dt, offset=offset)

        def fixed(name, shape, dt=F32):
            n = 4
            for s in shape[1:]:
                n *= s
            o = at[0]
            at[0] += (n + 31) // 32 * 32
            return place(name, shape, dt, o)

        K = 1024
        params = fixed("params", [P, N_PAR])
        ones = fixed("ones", [P, P])
        ident = fixed("ident", [P, P])
        zero = fixed("zero", [P, 1])
        eps = fixed("eps", [P, 1])
        cols = fixed("cols", [P, 2, 8])
        stat = fixed("stat", [P, 3, 8])
        w_raw = fixed("w_raw", [P, 2, T])
        w_hi = fixed("w_hi", [P, 2, T], F32R)
        w_lo = fixed("w_lo", [P, 2, T], F32R)
        h_hi = fixed("h_hi", [P, KT, T], F32R)
        h_lo = fixed("h_lo", [P, KT, T], F32R)
        X = at[0]
        A = X + 32 * K
        x = place("x", [P, KT, T], F32, X)
        hid_hi = place("hid_hi", [P, 2, 2, T], F32R, A)
        hid_lo = place("hid_lo", [P, 2, 2, T], F32R, A + 16 * K)
        silu = place("silu", [P, 2, T], F32, A + 32 * K)
        prod = place("prod", [P, 2, T], F32, A + 40 * K)
        sq = place("sq", [P, 2, T], F32, A + 48 * K)
        diag = place("diag", [P, T], F32, A + 48 * K)
        acc = place("acc", [P, T], F32, A + 56 * K)
        nt = place("nt", [P, 2, T], F32, A + 60 * K)
        M = A + 68 * K + 1536
        assert M + 16 * K <= nc.sbuf_usable_end
        mk_hi = place("mk_hi", [P, MH, MEM], F32R, M)
        mk_lo = place("mk_lo", [P, MH, MEM], F32R, M + 4 * K)
        mv_hi = place("mv_hi", [P, MT, MH * P], F32R, M + 8 * K)
        mv_lo = place("mv_lo", [P, MT, MH * P], F32R, M + 12 * K)
        mem_hi = place("mem_hi", [P, KT, MEM], F32R, M)
        mem_lo = place("mem_lo", [P, KT, MEM], F32R, M + 8 * K)
        mem = place("mem", [P, KT, MEM], F32, A)
        msq = place("msq", [P, 2, MEM], F32, A + 24 * K)
        mdiag = place("mdiag", [P, MEM], F32, A + 26 * K)
        macc = place("macc", [P, MEM], F32, A + 27 * K)
        mnt = place("mnt", [P, 2, MEM], F32, A + 28 * K)
        ext = place("ext", [HEADS, EXT], F32, A + 30 * K)
        ext_zero = place("ext_zero", [HEADS, EXT], F32, A + 33 * K)
        S0, S1 = X + 8 * K, A + 32 * K

        def both(name, shape, offset):
            return [place(f"{name}{n}", shape, F32R, s + offset * K) for n, s in enumerate((S0, S1))]

        q_hi, q_lo = both("q_hi", [P, T], 0), both("q_lo", [P, T], 4)
        k_hi, k_lo = both("k_hi", [P, T], 8), both("k_lo", [P, T], 12)
        v_hi, v_lo = both("v_hi", [P, KT, P], 16), both("v_lo", [P, KT, P], 20)
        vT = place("vT", [P, T], F32, X)
        o_hi = place("o_hi", [P, 4, T], F32R, A)
        o_lo = place("o_lo", [P, 4, T], F32R, A + 16 * K)
        bias = place("bias", [P, 2, BANDK], F32, A + 56 * K)
        pt_hi = place("pt_hi", [P, BANDK], F32R, A + 61 * K)
        pt_lo = place("pt_lo", [P, BANDK], F32R, A + 61 * K + 4 * BANDK)
        pr = [place("pr0", [P, BANDK], F32, X + 4 * K), place("pr1", [P, BANDK], F32, A + 66 * K)]
        gate = place("gate", [P, 2, T], F32, X)
        y = place("y", [P, KT, T], F32, A + 32 * K)
        SEG = PAD + T + 2
        conv = place("conv", [P, 5, SEG], F32, X + 32 * K - 5 * SEG * 4)
        c_hi = place("c_hi", [P, CT, T], F32R, A)
        c_lo = place("c_lo", [P, CT, T], F32R, A + 16 * K)
        mq_hi = place("mq_hi", [P, T], F32R, X)
        mq_lo = place("mq_lo", [P, T], F32R, X + 4 * K)
        mp = place("mp", [P, 2, 2, MEM], F32, A + 64 * K)
        c2 = X + 32 * K - 3 * SEG * 4
        mpt_hi = place("mpt_hi", [P, 2 * MEM], F32R, c2)
        mpt_lo = place("mpt_lo", [P, 2 * MEM], F32R, c2 + 2 * K)
        y_hi = place("y_hi", [P, KT, T], F32R, X - 64 * K)
        y_lo = place("y_lo", [P, KT, T], F32R, X - 32 * K)

        ln_sum = conv[:, 4, PAD:PAD + T]
        ln_sq = place("ln_sq", [P, 2, T], F32, M)
        ln_diag = place("ln_diag", [P, T], F32, M + 8 * K)

        ps = ctx.enter_context(nc.psum_tensor("ps", [P, 8 * HALF], F32))

        def bank(b, n=1):
            return ps[:, b * HALF:(b + n) * HALF]

        w_loaded = [sem("w_loaded0"), sem("w_loaded1")]
        w_rounded = sem("w_rounded")
        w_split = sem("w_split")
        w_used = sem("w_used")
        params_loaded = sem("params_loaded")
        rel_loaded = sem("rel_loaded")
        ext_stored = sem("ext_stored")
        rows_stored = sem("rows_stored")
        mem_loaded = sem("mem_loaded")
        x_loaded = [sem(f"x_loaded{k}") for k in range(KT)]
        const_ready = sem("const_ready")
        ext_zeroed = sem("ext_zeroed")
        ident_ready = sem("ident_ready")
        ext_ready = sem("ext_ready")
        x_spilled = sem("x_spilled")
        x_back = [sem(f"x_back{k}") for k in range(KT)]
        y_stored = sem("y_stored")

        class Norm:

            def __init__(self, sems, index):
                self.sems, self.index = sems, index
                self.squared = sems["squared"]
                self.summed = sems["summed"]
                self.cols_done = sems["cols_done"]
                self.std_done = sems["std_done"]
                self.rstd_done = sems["rstd_done"]
                self.diag_done = sems["diag_done"]
                self.spread = sems["spread"]
                self.scaled = sems["scaled"]
                self.hi_done = sems["hi_done"]
                self.lo_done = sems["lo_done"]

            def past(self, name, count):
                each = {"squared": KT, "summed": KT - 1, "scaled": KT, "hi_done": KT, "lo_done": KT}.get(name, 1)
                return self.sems[name], self.index * each + count

        def norm_sems(name):
            return {s: sem(f"{name}_{s}") for s in ("squared", "summed", "cols_done", "std_done", "rstd_done",
                                                    "diag_done", "spread", "scaled", "hi_done", "lo_done")}

        class Ffn:
            def __init__(self, name, unit):
                self.unit = unit
                self.up_done = sem(f"{name}_up_done")
                self.silu_done = sem(f"{name}_silu_done")
                self.prod_done = sem(f"{name}_prod_done")
                self.hi_done = sem(f"{name}_hi_done")
                self.lo_done = sem(f"{name}_lo_done")
                self.down_done = sem(f"{name}_down_done")
                self.acc_done = sem(f"{name}_acc_done")

        class Gated:
            def __init__(self, name, unit):
                self.unit = unit
                self.gate_done = sem(f"{name}_gate_done")
                self.sig_done = sem(f"{name}_sig_done")
                self.branch_done = sem(f"{name}_branch_done")
                self.y_done = sem(f"{name}_y_done")
                self.mul_done = sem(f"{name}_mul_done")

        of_x = norm_sems("norm")
        n_mem, n_ffn1, n_mix, n_ffn2, n_fin = [Norm(of_x, i) for i in range(5)]
        n_ln = Norm(norm_sems("layer_norm"), 0)
        f1, f2 = Ffn("f1", U_FFN1), Ffn("f2", U_FFN2)
        g_att, g_mem, g_conv = Gated("gatt", U_ATT), Gated("gmem", U_MEMO), Gated("gconv", U_CONVO)
        kv_done, kv_hi, kv_lo = sem("kv_done"), sem("kv_hi"), sem("kv_lo")
        qkv_done, qkv_hi, qkv_lo = sem("qkv_done"), sem("qkv_hi"), sem("qkv_lo")
        vt_copied, vt_turned, v_hi_done, v_lo_done = sem("vt_copied"), sem("vt_turned"), sem("v_hi_done"), sem("v_lo_done")
        bias_in, bias_masked = [sem("bias_in0"), sem("bias_in1")], sem("bias_masked")
        ag_done, ag_copied = sem("ag_done"), sem("ag_copied")

        class Att:
            def __init__(self, name):
                self.qk_done = sem(f"{name}_qk_done")
                self.max_done = sem(f"{name}_max_done")
                self.exp_done = sem(f"{name}_exp_done")
                self.rcp_done = sem(f"{name}_rcp_done")
                self.norm_done = sem(f"{name}_norm_done")
                self.turned = sem(f"{name}_turned")
                self.pt_hi_done = sem(f"{name}_pt_hi_done")
                self.pt_lo_done = sem(f"{name}_pt_lo_done")
                self.pv_done = sem(f"{name}_pv_done")
                self.o_hi_done = sem(f"{name}_o_hi_done")
                self.o_lo_done = sem(f"{name}_o_lo_done")

        at_c, at_m = Att("catt"), Att("matt")
        mq_done, mq_hi_done, mq_lo_done = sem("mq_done"), sem("mq_hi_done"), sem("mq_lo_done")
        glu_done, glu_sig, glu_v, pad_done = sem("glu_done"), sem("glu_sig"), sem("glu_v"), sem("pad_done")
        dw_done = sem("dw_done")
        ln_mean_in, ln_mean_done = sem("nln_mean_in"), sem("nln_mean_done")
        ln_centred, ln_silu_done = sem("nln_centred"), sem("nln_silu_done")
        y_hi_done, y_lo_done = sem("y_hi_done"), sem("y_lo_done")
        out_done, x_added = sem("out_done"), sem("x_added")

        def key_width(j):
            return min(j + 1, 5) * P

        N_ITEMS = 64
        SECOND_TURNS = (0, 17, 33, 49)
        score_at, turn_at = 2 * HALF, 4 * HALF
        item_out = bank(6)[:, 0:P]

        def item(n):
            t, m = n // 16, n % 16
            j = m % 8
            return t, t % 2, m // 8, j, key_width(j), max(j - 4, 0) * P

        def fill(n):
            t, m = n // 16, n % 16
            return range(3 * m, 3 * m + 3) if t < 3 else range(4 * m, 4 * m + 4)

        def halves_done(n):
            return [p // 8 for p in fill(n) if p % 8 == 7]

        block = ctx.enter_context(nc.Block())

        @block.sync
        def _(sp):
            for s in range(2):
                sp.dma_start(w_raw[:, s, :], weights[s]).then_inc(w_loaded[s], 16)
            with sp.Fori(1, UNITS // 2) as i:
                for s in range(2):
                    sp.wait_ge(w_split, 2 * i + (s - 1))
                    sp.dma_start(w_raw[:, s, :], weights[2 * i + s]).then_inc(w_loaded[s], 16)

        @block.gpsimd
        def _(pool):
            nc.gpsimd.memset(zero[:], 0.0).then_inc(const_ready, 1)
            nc.gpsimd.memset(eps[:], EPS).then_inc(const_ready, 1)
            nc.gpsimd.memset(ones[:], 1.0).then_inc(const_ready, 1)
            nc.gpsimd.memset(ident[:], 0.0).then_inc(const_ready, 1)
            pool.wait_ge(const_ready, 4)
            nc.gpsimd.affine_select(out=ident[:], in_=ident[:], compare_op=ALU.not_equal, fill=1.0, base=0,
                                    pattern=[[-1, P]], channel_multiplier=1).then_inc(ident_ready, 1)

            def cut(s, loaded, rounded):
                pool.wait_ge(w_loaded[s], loaded)
                nc.gpsimd.tensor_tensor(w_hi[:, s, :], w_raw[:, s, :], zero[:].to_broadcast([P, T]),
                                        ALU.add).then_inc(w_rounded, 1)
                pool.wait_ge(w_rounded, rounded)
                nc.gpsimd.tensor_tensor(w_lo[:, s, :], w_raw[:, s, :], w_hi[:, s, :].bitcast(F32),
                                        ALU.subtract).then_inc(w_split, 1)

            for s in range(2):
                cut(s, 16, s + 1)
            with pool.Fori(1, UNITS // 2) as i:
                for s in range(2):
                    pool.wait_ge(w_used, 2 * i + (s - 1))
                    cut(s, 16 * i + 16, 2 * i + (s + 1))

        @block.tensor
        def _(pe):
            release = [False]

            def unit(u, first=False):
                slot = u % 2 if isinstance(u, int) else None
                pe.wait_ge(w_split, u + 1)
                release[0] = not first
                return slot

            def step(out, stationary, moving, start, stop):
                (sh, sl), (mh, ml) = stationary, moving
                mm = nc.tensor.matmul(out, sh, mh, start=start, stop=False)
                if release[0]:
                    mm.then_inc(w_used, 1)
                    release[0] = False
                nc.tensor.matmul(out, sh, ml, start=False, stop=False)
                return nc.tensor.matmul(out, sl, mh, start=False, stop=stop)

            def weight(slot, at_col):
                return w_hi[:, slot, at_col:at_col + P], w_lo[:, slot, at_col:at_col + P]

            def dense(outs, slot, src, ks, done, each=False, off=0, width=P, before=None):
                for half, out in enumerate(outs):
                    for n, k in enumerate(ks):
                        if before is not None and half == 0:
                            before(k)
                        mm = step(out, weight(slot, off + n * width), src(k, half), n == 0, n == len(ks) - 1)
                    if each or half == len(outs) - 1:
                        mm.then_inc(done, 1)

            def dense_two(u, outs, src, done, before):
                lag = 2
                for n in range(KT + lag):
                    if n < KT:
                        before(n)
                    for slot, k in ((0, n), (1, n - lag)):
                        if not 0 <= k < KT:
                            continue
                        if slot == 1 and k == 0:
                            pe.wait_ge(w_split, u + 2)
                        if slot == 1 and n == KT:
                            release[0] = True
                        for half in range(2):
                            mm = step(outs[slot][half], weight(slot, k * P), src(k, half), k == 0, k == KT - 1)
                        if k == KT - 1:
                            mm.then_inc(done, 1)

            def rows(hi, lo):
                def src(k, half):
                    a = slice(half * HALF, (half + 1) * HALF)
                    return hi[:, k, a], lo[:, k, a]
                return src

            def pair(slot):
                return [bank(2 * slot), bank(2 * slot + 1)]

            def norm_cols(n, a, count, width=T):
                pe.wait_ge(*n.past("summed", count))
                for i in range(width // P):
                    mm = nc.tensor.matmul(bank(4)[:, i:i + 1], a[:, i * P:(i + 1) * P], ones[:, 0:1],
                                          start=True, stop=True)
                    if release[0]:
                        mm.then_inc(w_used, 1)
                        release[0] = False
                mm.then_inc(n.cols_done, 1)

            def norm_spread(n, dg, width=T):
                pe.wait_ge(*n.past("diag_done", 1))
                for i in range(width // P):
                    mm = nc.tensor.matmul(ps[:, 6 * HALF + i * P:6 * HALF + (i + 1) * P], ones[:],
                                          dg[:, i * P:(i + 1) * P], start=True, stop=True)
                mm.then_inc(n.spread, 1)

            pe.wait_ge(const_ready, 4)
            norm_cols(n_mem, macc, KT - 1, MEM)
            norm_spread(n_mem, mdiag, MEM)

            def memory_product(c):
                slot = unit(U_KV + c)
                if c % 4 == 0:
                    pe.wait_ge(f1.acc_done, 8 * (PAIRS - 1) + 5 + c // 4)
                b = bank(c // 2)[:, (c % 2) * MEM:(c % 2 + 1) * MEM]
                for m in range(1 if c < MH else MT):
                    for k in range(KT):
                        if c < MH:
                            mm = step(b, weight(slot, k * P), (mem_hi[:, k, :], mem_lo[:, k, :]), k == 0, k == KT - 1)
                        else:
                            a = slice(m * P, (m + 1) * P)
                            mm = step(b[:, a], (mem_hi[:, k, a], mem_lo[:, k, a]), weight(slot, k * P),
                                      k == 0, k == KT - 1)
                mm.then_inc(kv_done, 1)

            def ffn(f, n):
                def up(base, slot_free, span=range(4)):
                    for s in span:
                        slot = unit_in(base, s)
                        if slot_free is not None:
                            pe.wait_ge(*slot_free(s))
                        dense(pair(s), slot, rows(h_hi, h_lo), range(KT), f.up_done)

                def down(base, par, slot_free):
                    for d in range(KT):
                        if d % 4 == 0:
                            slot = unit_in(base, d // 4)
                        pe.wait_ge(*slot_free(d))
                        dense(pair(d % 4), slot, rows(hid_hi[:, par], hid_lo[:, par]), range(2), f.down_done,
                              off=(d % 4) * P, width=4 * P)

                def unit_in(base, s):
                    unit(base + s)
                    return s % 2

                def turn(i, first):
                    for r in range(2):
                        base = f.unit + 4 + 12 * i + 6 * r
                        if first and r == 0:
                            up(base, lambda s: (f.prod_done, s // 2 + 1))
                        else:
                            up(base, lambda s: (f.acc_done, 16 * i + (8 * r - 3 + s)))
                        pe.wait_ge(f.lo_done, 4 * i + (2 * r + 2))
                        down(base + 4, r, lambda d: (f.prod_done, 4 * i + (2 * r + 3 + d // 2)) if d < 4
                             else (f.acc_done, 16 * i + (8 * r + d - 3)))

                unit(f.unit, first=True)
                dense_two(f.unit, (pair(0), pair(1)), rows(h_hi, h_lo), f.up_done,
                          lambda k: pe.wait_ge(*n.past("lo_done", k + 1)))
                up(f.unit, None, range(2, 4))
                turn(0, True)
                with pe.Fori(1, (PAIRS - 1) // 2) as i:
                    turn(i, False)
                pe.wait_ge(f.lo_done, 2 * PAIRS)
                down(f.unit + 6 * PAIRS - 2, (PAIRS - 1) % 2, lambda d: (f.acc_done, 8 * (PAIRS - 1) + d - 3))

            norm_cols(n_ffn1, acc, KT - 1)
            norm_spread(n_ffn1, diag)
            ffn(f1, n_ffn1)

            memory_product(0)
            norm_cols(n_mix, acc, KT - 1)
            memory_product(1)
            norm_spread(n_mix, diag)
            for c in range(2, 2 * MH):
                memory_product(c)

            def project(t, p):
                c, half, k = p // 16, p // 8 % 2, p % 8
                u = U_QKV + 3 * t + c
                if p % 16 == 0:
                    unit(u)
                if k == 0:
                    if c > 0:
                        pe.wait_ge(qkv_lo, 4 * t + 2 * c - 1 + half)
                    elif t > 0:
                        pe.wait_ge(vt_copied, 2 * t - 1 + half)
                    else:
                        pe.wait_ge(kv_lo, 2)
                if t == 0 and p < KT:
                    pe.wait_ge(*n_mix.past("lo_done", k + 1))
                mm = step(bank(half), weight(u % 2, k * P), rows(h_hi, h_lo)(k, half), k == 0, k == KT - 1)
                if k == KT - 1:
                    mm.then_inc(qkv_done, 1)

            def conv_part(p):
                c, half, k = p // 16, p // 8 % 2, p % 8
                u = U_CONV + c
                if p % 16 == 0:
                    unit(u)
                if k == 0:
                    if c > 0:
                        pe.wait_ge(ag_copied, 2 * c - 1 + half)
                    else:
                        pe.wait_ge(vt_copied, 7 + half)
                mm = step(bank(half), weight(u % 2, k * P), rows(h_hi, h_lo)(k, half), k == 0, k == KT - 1)
                if k == KT - 1:
                    mm.then_inc(ag_done, 1)

            def turn_values(t, half):
                pe.wait_ge(vt_copied, 2 * t + half + 1)
                if 2 * t + half > 0:
                    pe.wait_ge(v_lo_done, 2 * t + half)
                for i in range(4):
                    c = 4 * half + i
                    mm = nc.tensor.transpose(bank(7)[:, i * P:(i + 1) * P], vT[:, c * P:(c + 1) * P], ident[:])
                mm.then_inc(vt_turned, 1)

            def scores(n):
                t, b, e, j, w, key = item(n)
                if n % 16 == 0:
                    pe.wait_ge(qkv_lo, 4 * t + 4)
                if n > 0:
                    pe.wait_ge(at_c.max_done, n)
                r, qs = slice(64 * e, 64 * e + 64), slice(j * P, (j + 1) * P)
                for c in range(0, w, HALF):
                    size = min(HALF, w - c)
                    ks = slice(key + c, key + c + size)
                    mm = step(ps[:, score_at + c:score_at + c + size], (q_hi[b][r, qs], q_lo[b][r, qs]),
                              (k_hi[b][r, ks], k_lo[b][r, ks]), True, True)
                mm.then_inc(at_c.qk_done, 1)

            def turn_probs(n):
                w = item(n)[4]
                pe.wait_ge(at_c.norm_done, n + 1)
                if n > 0:
                    pe.wait_ge(at_c.pt_lo_done, n)
                for i in range(w // P):
                    mm = nc.tensor.transpose(ps[:, turn_at + i * P:turn_at + (i + 1) * P],
                                             pr[n % 2][:, i * P:(i + 1) * P], ident[:])
                mm.then_inc(at_c.turned, 1)

            def values(n):
                t, b, e, j, w, key = item(n)
                pe.wait_ge(at_c.pt_lo_done, n + 1)
                if n % 8 == 0:
                    pe.wait_ge(v_lo_done, 2 * t + 2)
                if n > 0:
                    pe.wait_ge(at_c.o_lo_done, n)
                for i in range(w // P):
                    kt, a = key // P + i, slice(i * P, (i + 1) * P)
                    mm = step(item_out, (v_hi[b][:, kt, :], v_lo[b][:, kt, :]), (pt_hi[:, a], pt_lo[:, a]),
                              i == 0, i == w // P - 1)
                mm.then_inc(at_c.pv_done, 1)

            for p in range(48):
                project(0, p)
            turn_values(0, 0)
            for n in range(N_ITEMS + 1):
                t, m = n // 16, n % 16
                if n < N_ITEMS:
                    scores(n)
                if n > 0:
                    turn_probs(n - 1)
                if m == 15:
                    if t < 3:
                        turn_values(t + 1, 0)
                elif n in SECOND_TURNS:
                    turn_values(t, 1)
                if n < N_ITEMS:
                    for p in fill(n):
                        project(t + 1, p) if t < 3 else conv_part(p)
                if n > 0:
                    values(n - 1)

            for c in range(4):
                slot = unit(U_CONV + 4 + c)
                if c == 0:
                    pe.wait_ge(ag_copied, 8)
                elif c == 1:
                    pe.wait_ge(at_c.max_done, N_ITEMS)
                elif c == 2:
                    pe.wait_ge(at_c.pt_lo_done, N_ITEMS)
                else:
                    pe.wait_ge(at_c.o_lo_done, N_ITEMS)
                dense(pair(c), slot, rows(h_hi, h_lo), range(KT), glu_done)

            def gates(g, base, u, s, slot):
                unit(u)
                pe.wait_ge(g.y_done, base + s + 1)
                dense(pair(s), slot, rows(h_hi, h_lo), range(KT), g.gate_done)

            def branch(g, base, s, slot, src):
                pe.wait_ge(g.sig_done, base + s + 1)
                dense(pair(s), slot, src, range(CT), g.branch_done, off=s * P, width=2 * P)

            pe.wait_ge(glu_v, 3)
            with pe.Fori(0, 2) as i:
                for r in range(2):
                    u = U_ATT + 6 * i + 3 * r
                    base = 4 * i + 2 * r
                    for s in range(2):
                        gates(g_att, base, u + s, s, (r + s) % 2)
                    unit(u + 2)
                    for s in range(2):
                        branch(g_att, base, s, r % 2, rows(o_hi, o_lo))

            def m_query(h, p):
                half, k = p // 8, p % 8
                u = U_MQ + h
                if p == 0:
                    unit(u)
                if k == 0:
                    if h >= 1:
                        pe.wait_ge(mq_lo_done, 2 * h - 1 + half)
                    else:
                        pe.wait_ge(g_att.y_done, KT + 2)
                mm = step(bank(half), weight(u % 2, k * P), rows(h_hi, h_lo)(k, half), k == 0, k == KT - 1)
                if h < MH and k == KT - 1:
                    mm.then_inc(mq_done, 1)
                elif p == 15:
                    mm.then_inc(g_mem.gate_done, 1)

            def m_scores(n):
                h, i = n // 4, n % 4
                pe.wait_ge(mq_lo_done, 2 * h + i // 2 + 1)
                if n >= 2:
                    pe.wait_ge(at_m.exp_done, n - 1)
                for q in range(2):
                    a = slice((2 * i + q) * P, (2 * i + q + 1) * P)
                    mm = step(bank(4 + n % 2)[:, q * MEM:(q + 1) * MEM], (mq_hi[:, a], mq_lo[:, a]),
                              (mk_hi[:, h, :], mk_lo[:, h, :]), True, True)
                mm.then_inc(at_m.qk_done, 1)

            def m_turn(n):
                pe.wait_ge(at_m.norm_done, n + 1)
                if n >= 2:
                    pe.wait_ge(at_m.pt_lo_done, n - 1)
                for kt in range(MT):
                    for q in range(2):
                        a = kt * MEM + q * P
                        mm = nc.tensor.transpose(bank(6 + n % 2)[:, a:a + P], mp[:, n % 2, q, kt * P:(kt + 1) * P], ident[:])
                mm.then_inc(at_m.turned, 1)

            def m_values(n):
                h = n // 4
                pe.wait_ge(at_m.pt_lo_done, n + 1)
                if n >= 2:
                    pe.wait_ge(at_m.o_lo_done, n - 1)
                for kt in range(MT):
                    a, b = slice(h * P, (h + 1) * P), slice(kt * MEM, (kt + 1) * MEM)
                    mm = step(bank(2 + n % 2)[:, 0:MEM], (mv_hi[:, kt, a], mv_lo[:, kt, a]), (mpt_hi[:, b], mpt_lo[:, b]),
                              kt == 0, kt == MT - 1)
                mm.then_inc(at_m.pv_done, 1)

            for p in range(16):
                m_query(0, p)
            for n in range(16 + 1):
                h, i = n // 4, n % 4
                if i > 0:
                    m_scores(n)
                if n > 0:
                    m_turn(n - 1)
                for p in ((), range(0, 5), range(5, 10), range(10, 16))[i]:
                    m_query(h + 1, p)
                if n > 0:
                    m_values(n - 1)
                if i == 0 and n < 16:
                    m_scores(n)

            for dp in range(4):
                u = U_MEMO + 3 * dp
                for s in range(2):
                    if dp == 0 and s == 1:
                        pe.wait_ge(at_m.o_lo_done, 16)
                    if dp > 0 or s == 1:
                        gates(g_mem, 2 * dp, u + s, s, (u + s) % 2)
                    if dp == 3 and s == 0:
                        pe.wait_ge(ln_mean_in, CT - 1)
                        for half in range(2):
                            mm = nc.tensor.matmul(bank(4 + half), ones[:], ln_sum[:, half * HALF:(half + 1) * HALF],
                                                  start=True, stop=True)
                        mm.then_inc(ln_mean_done, 1)
                    if dp == 3 and s == 1:
                        norm_cols(n_ln, ln_sum, CT - 1)
                unit(u + 2)
                for s in range(2):
                    branch(g_mem, 2 * dp, s, (u + 2) % 2, rows(o_hi, o_lo))
                    if dp == 3 and s == 0:
                        norm_spread(n_ln, ln_diag)

            for dp in range(4):
                u = U_CONVO + 3 * dp
                for s in range(2):
                    if dp == 0:
                        pe.wait_ge(g_mem.mul_done, KT - 1 + s)
                    gates(g_conv, 2 * dp, u + s, s, (u + s) % 2)
                if dp == 0:
                    pe.wait_ge(*n_ln.past("lo_done", CT))
                unit(u + 2)
                for s in range(2):
                    branch(g_conv, 2 * dp, s, (u + 2) % 2, rows(c_hi, c_lo))

            unit(U_OUT)
            dense_two(U_OUT, (pair(0), pair(1)), rows(y_hi, y_lo), out_done, lambda k: pe.wait_ge(y_lo_done, k + 1))
            for d in range(2, KT):
                slot = unit(U_OUT + d)
                if d >= 4:
                    pe.wait_ge(x_added, d - 3)
                dense(pair(d % 4), slot, rows(y_hi, y_lo), range(KT), out_done)

            release[0] = True
            norm_cols(n_ffn2, acc, KT - 1)
            norm_spread(n_ffn2, diag)
            ffn(f2, n_ffn2)
            norm_cols(n_fin, acc, KT - 1)
            norm_spread(n_fin, diag)

        @block.scalar
        def _(act):
            act.dma_start(mem[:], mem_in).then_inc(mem_loaded, 16)
            act.dma_start(params[:], params_in).then_inc(params_loaded, 16)
            for k in range(KT):
                act.dma_start(x[:, k, :], x_in[k]).then_inc(x_loaded[k], 16)
            act.wait_ge(ext_zeroed, 1)
            act.dma_start(ext[:, EXT - 257:EXT - 257 + REL], rel_in).then_inc(rel_loaded, 16)

            def copy(out, in_, done, scale=1.0):
                nc.scalar.activation(out, in_, ACT.Copy, scale=scale).then_inc(done, 1)

            def squares(n, src, buf, ready):
                for k in range(KT):
                    ready(k)
                    if k >= 2:
                        act.wait_ge(*n.past("summed", max(1, k - 2)))
                    nc.scalar.activation(buf[:, k % 2, :], src[:, k, :], ACT.Square).then_inc(n.squared, 1)

            def deviation(n, width=T, channels=D):
                act.wait_ge(*n.past("cols_done", 1))
                nc.scalar.activation(cols[:, 0, 0:width // P], bank(4)[:, 0:width // P], ACT.Sqrt, bias=eps[:],
                                     scale=1.0 / channels).then_inc(n.std_done, 1)

            def round_rows(n, dst, buf):
                for k in range(KT):
                    act.wait_ge(*n.past("scaled", k + 1))
                    copy(dst[:, k, :], buf[:, k % 2, :], n.hi_done)

            squares(n_mem, mem, msq, lambda k: act.wait_ge(mem_loaded, 16))
            act.wait_ge(const_ready, 4)
            deviation(n_mem, MEM)
            round_rows(n_mem, mem_hi, mnt)
            squares(n_ffn1, x, sq, lambda k: act.wait_ge(x_loaded[k], 16))
            act.wait_ge(ext_ready, 1)
            act.dma_start(rel_ext.ap(), ext[:]).then_inc(ext_stored, 16)
            act.wait_ge(ext_stored, 16)
            act.dma_start(bias_rows,
                          bass.AP(rel_ext, P - 1, [[EXT, HEADS], [-1, P], [1, BANDK]])).then_inc(rows_stored, 16)

            def ffn(f):
                def tile(F, par, ff, first):
                    act.wait_ge(f.up_done, 2 * F + 1)
                    if not first:
                        act.wait_ge(f.prod_done, F - 1)
                    nc.scalar.activation(silu[:, ff, :], bank(4 * ff, 2), ACT.Silu).then_inc(f.silu_done, 1)

                def round_hidden(F, par, ff, used):
                    act.wait_ge(f.prod_done, F + 1)
                    if used is not None:
                        act.wait_ge(f.down_done, used)
                    copy(hid_hi[:, par, ff, :], prod[:, ff, :], f.hi_done)

                for ff in range(2):
                    tile(ff, 0, ff, True)
                    round_hidden(ff, 0, ff, None)

                def turn(i, first):
                    for r in range(2):
                        for ff in range(2):
                            F = 4 * i + (2 + 2 * r + ff)
                            tile(F, 1 - r, ff, False)
                            round_hidden(F, 1 - r, ff, None if first and r == 0 else 16 * i + 8 * r)

                turn(0, True)
                with act.Fori(1, (PAIRS - 1) // 2) as i:
                    turn(i, False)

            deviation(n_ffn1)
            round_rows(n_ffn1, h_hi, nt)
            ffn(f1)

            def x_ready(f):
                def ready(k):
                    act.wait_ge(f.acc_done, 8 * (PAIRS - 1) + k + 1)
                return ready

            squares(n_mix, x, sq, x_ready(f1))
            for k in range(KT):
                act.dma_start(x_spill[k], x[:, k, :]).then_inc(x_spilled, 16)
            deviation(n_mix)
            round_rows(n_mix, h_hi, nt)

            act.wait_ge(kv_done, 2 * MH)
            copy(mk_hi[:], bank(0, 2).rearrange("p (h k) -> p h k", h=MH), kv_hi)
            copy(mv_hi[:].rearrange("p m (h d) -> p h m d", h=MH), bank(2, 2).rearrange("p (h m d) -> p h m d", h=MH, m=MT), kv_hi)

            act.wait_ge(x_spilled, 16 * KT)
            act.wait_ge(*n_mix.past("lo_done", KT))
            act.wait_ge(rows_stored, 16)

            def load_bias(h):
                if h >= 2:
                    act.wait_ge(at_c.max_done, 8 * (h - 1))
                act.dma_start(bias[:, h % 2, :], bias_rows[h]).then_inc(bias_in[h % 2], 16)

            def round_half(t, c):
                which, half = c // 2, c % 2
                a, b = slice(half * HALF, (half + 1) * HALF), t % 2
                act.wait_ge(qkv_done, 6 * t + c + 1)
                if which == 2:
                    if t >= 1:
                        act.wait_ge(vt_turned, 2 * t - 1 + half)
                    copy(vT[:, a], bank(half), vt_copied)
                else:
                    if t >= 2:
                        act.wait_ge(at_c.qk_done, 16 * (t - 1))
                    copy((q_hi, k_hi)[which][b][:, a], bank(half), qkv_hi, scale=(DH ** -0.5, 1.0)[which])

            def round_values(t, half):
                act.wait_ge(vt_turned, 2 * t + half + 1)
                if t >= 2:
                    act.wait_ge(at_c.pv_done, 16 * (t - 1))
                copy(v_hi[t % 2][:, 4 * half:4 * half + 4, :], bank(7).rearrange("p (c d) -> p c d", c=4), v_hi_done)

            def copy_input(c):
                half = c % 2
                dst = (conv[:, 1, :], gate[:, 0, :], conv[:, 2, :], conv[:, 0, :])[c // 2]
                at_col = half * HALF + (0 if c // 2 == 1 else PAD)
                act.wait_ge(ag_done, c + 1)
                if c == 0:
                    act.wait_ge(at_c.pv_done, 48)
                    act.wait_ge(vt_turned, 8)
                copy(dst[:, at_col:at_col + HALF], bank(half), ag_copied)

            def exps(n):
                w = item(n)[4]
                act.wait_ge(at_c.max_done, n + 1)
                nc.scalar.activation(pr[n % 2][:, 0:w], pr[n % 2][:, 0:w], ACT.Exp, bias=stat[:, 0, n % 2:n % 2 + 1],
                                     scale=-1.0, accum_out=stat[:, 1, n % 2:n % 2 + 1]).then_inc(at_c.exp_done, 1)

            def round_probs(n):
                w = item(n)[4]
                act.wait_ge(at_c.turned, n + 1)
                if n > 0:
                    act.wait_ge(at_c.pv_done, n)
                copy(pt_hi[:, 0:w], ps[:, turn_at:turn_at + w], at_c.pt_hi_done)

            def round_out(n):
                t, b, e, j, w, key = item(n)
                act.wait_ge(at_c.pv_done, n + 1)
                r = slice(64 * e, 64 * e + 64)
                copy(o_hi[r, t, j * P:(j + 1) * P], item_out[r, :], at_c.o_hi_done)

            load_bias(0)
            load_bias(1)
            for c in range(6):
                round_half(0, c)
            round_values(0, 0)
            for n in range(N_ITEMS + 1):
                t, m = n // 16, n % 16
                if n > 0:
                    round_probs(n - 1)
                if n < N_ITEMS:
                    exps(n)
                if m == 15 and t < 3:
                    round_values(t + 1, 0)
                elif n in SECOND_TURNS:
                    round_values(t, 1)
                if n < N_ITEMS:
                    for c in halves_done(n):
                        round_half(t + 1, c) if t < 3 else copy_input(c)
                if n > 0:
                    round_out(n - 1)
                if n % 8 == 7 and n // 8 + 2 < HEADS:
                    load_bias(n // 8 + 2)

            for t in range(CT):
                if t < 2:
                    act.wait_ge(ag_copied, 8)
                    g = (gate[:, 0, :], conv[:, 0, PAD:PAD + T])[t]
                    nc.scalar.activation(g, g, ACT.Sigmoid).then_inc(glu_sig, 1)
                else:
                    act.wait_ge(glu_done, 2 * (t - 2) + 2)
                    if t == 3:
                        act.wait_ge(glu_v, 1)
                    nc.scalar.activation(gate[:, 3 - t, :], bank(4 * (t - 2) + 2, 2), ACT.Sigmoid).then_inc(glu_sig, 1)

            def sigmoids(g, base, s, col):
                act.wait_ge(g.gate_done, base + s + 1)
                act.wait_ge(g.y_done, base + s + 1)
                nc.scalar.activation(gate[:, s, :], bank(2 * s, 2), ACT.Sigmoid, bias=params[:, bass.ds(col, 1)]
                                     if not isinstance(col, int) else params[:, col:col + 1]).then_inc(g.sig_done, 1)

            act.wait_ge(glu_v, CT)
            with act.Fori(0, 4) as dp:
                for s in range(2):
                    sigmoids(g_att, 2 * dp, s, C_GATE + KT + 2 * dp + s)

            act.wait_ge(g_att.y_done, KT + 2)

            def m_query(h):
                for half in range(2):
                    act.wait_ge(mq_done, 2 * h + half + 1)
                    if h >= 1 and half == 0:
                        act.wait_ge(at_m.qk_done, 4 * h)
                    copy(mq_hi[:, half * HALF:(half + 1) * HALF], bank(half), mq_hi_done, scale=P ** -0.5)

            def m_exps(n):
                act.wait_ge(at_m.max_done, n + 1)
                if n >= 2:
                    act.wait_ge(at_m.turned, n - 1)
                for q in range(2):
                    c = 2 * (n % 2) + q
                    e = nc.scalar.activation(mp[:, n % 2, q, :], bank(4 + n % 2)[:, q * MEM:(q + 1) * MEM], ACT.Exp,
                                             bias=stat[:, 0, c:c + 1], accum_out=stat[:, 1, c:c + 1])
                e.then_inc(at_m.exp_done, 1)

            def m_round_probs(n):
                act.wait_ge(at_m.turned, n + 1)
                if n >= 1:
                    act.wait_ge(at_m.pv_done, n)
                copy(mpt_hi[:], bank(6 + n % 2), at_m.pt_hi_done)

            def m_round_out(n):
                act.wait_ge(at_m.pv_done, n + 1)
                copy(o_hi[:, n // 4, (n % 4) * MEM:(n % 4 + 1) * MEM], bank(2 + n % 2)[:, 0:MEM], at_m.o_hi_done)

            m_query(0)
            for n in range(16 + 1):
                if n > 0:
                    m_round_probs(n - 1)
                if 0 < n < 16 and n % 4 == 0:
                    m_query(n // 4)
                    m_round_out(n - 1)
                    m_exps(n)
                else:
                    if n < 16:
                        m_exps(n)
                    if n > 0:
                        m_round_out(n - 1)

            def ln_squares():
                for c in range(CT):
                    act.wait_ge(ln_centred, c + 1)
                    if c >= 2:
                        act.wait_ge(*n_ln.past("summed", max(1, c - 2)))
                    nc.scalar.activation(ln_sq[:, c % 2, :], conv[:, c, PAD:PAD + T], ACT.Square).then_inc(n_ln.squared, 1)

            for dp in range(4):
                for s in range(2):
                    sigmoids(g_mem, 2 * dp, s, C_GATE + 2 * KT + 2 * dp + s)
                    if dp == 3 and s == 0:
                        ln_squares()
            deviation(n_ln, channels=CONV)

            def ln_out():
                for c in range(CT):
                    act.wait_ge(*n_ln.past("scaled", c + 1))
                    nc.scalar.activation(conv[:, c, PAD:PAD + T], conv[:, c, PAD:PAD + T], ACT.Silu,
                                         bias=params[:, C_LNB + c:C_LNB + c + 1]).then_inc(ln_silu_done, 1)
                    act.wait_ge(ln_silu_done, c + 1)
                    act.wait_ge(g_mem.branch_done, KT)
                    copy(c_hi[:, c, :], conv[:, c, PAD:PAD + T], n_ln.hi_done)

            ln_out()
            for dp in range(4):
                for s in range(2):
                    if dp == 0:
                        act.wait_ge(g_mem.y_done, KT + 1 + s)
                    sigmoids(g_conv, 2 * dp, s, C_GATE + 2 * dp + s)

            act.wait_ge(g_conv.gate_done, KT)
            for k in range(KT):
                act.wait_ge(g_conv.y_done, 2 + k + 1)
                copy(y_hi[:, k, :], y[:, k, :], y_hi_done)
            for k in range(KT):
                act.dma_start(x[:, k, :], x_spill[k]).then_inc(x_back[k], 16)

            squares(n_ffn2, x, sq, lambda k: act.wait_ge(x_added, k + 1))
            deviation(n_ffn2)
            round_rows(n_ffn2, h_hi, nt)
            ffn(f2)
            squares(n_fin, x, sq, x_ready(f2))
            deviation(n_fin)
            for k in range(KT):
                act.wait_ge(*n_fin.past("scaled", k + 1))
                act.dma_start(y_out[k], x[:, k, :]).then_inc(y_stored, 16)
            act.wait_ge(y_stored, 16 * KT)

        @block.vector
        def _(dve):
            dve.sem_inc(dw_done, 1)
            for g in (g_att, g_mem, g_conv):
                dve.sem_inc(g.y_done, 2)

            def cut(out, whole, hi, done):
                nc.vector.tensor_tensor(out, whole, hi.bitcast(F32), ALU.subtract).then_inc(done, 1)

            def add_squares(n, buf, a, count, k):
                if k == 0:
                    return
                dve.wait_ge(*n.past("squared", k + 1))
                if k == 1:
                    nc.vector.tensor_tensor(a, buf[:, 0, :], buf[:, 1, :], ALU.add).then_inc(n.summed, 1)
                else:
                    dve.wait_ge(*n.past("summed", k - 1))
                    nc.vector.tensor_tensor(a, a, buf[:, k % 2, :], ALU.add).then_inc(n.summed, 1)

            def factors(n, dg, width=T):
                w = width // P
                dve.wait_ge(*n.past("std_done", 1))
                nc.vector.reciprocal(cols[:, 1, 0:w], cols[:, 0, 0:w]).then_inc(n.rstd_done, 1)
                dve.wait_ge(*n.past("rstd_done", 1))
                for i in range(w):
                    d = nc.vector.tensor_scalar(dg[:, i * P:(i + 1) * P], ident[:], cols[:, 1, i:i + 1], None, ALU.mult)
                d.then_inc(n.diag_done, 1)

            def scale(n, out, src, gain, width=T):
                nc.vector.scalar_tensor_tensor(out=out, in0=src, scalar=params[:, gain:gain + 1],
                                               in1=ps[:, 6 * HALF:6 * HALF + width], op0=ALU.mult,
                                               op1=ALU.mult).then_inc(n.scaled, 1)

            def normalise(n, src, buf, gain, lo, hi, width=T):
                dve.wait_ge(*n.past("spread", 1))
                for k in range(KT + 1):
                    if k < KT:
                        if k >= 2:
                            dve.wait_ge(*n.past("lo_done", k - 1))
                        scale(n, buf[:, k % 2, :], src[:, k, :], gain + k, width)
                    if k >= 1:
                        dve.wait_ge(*n.past("hi_done", k))
                        cut(lo[:, k - 1, :], buf[:, (k - 1) % 2, :], hi[:, k - 1, :], n.lo_done)

            nc.vector.memset(ext[:], 0.0).then_inc(ext_zeroed, 1)
            nc.vector.memset(ext_zero[:], 0.0).then_inc(ext_zeroed, 1)
            for k in range(KT):
                add_squares(n_mem, msq, macc[:], KT, k)
            dve.wait_ge(ident_ready, 1)
            factors(n_mem, mdiag, MEM)
            dve.wait_ge(params_loaded, 16)
            normalise(n_mem, mem, mnt, C_MEM, mem_lo, mem_hi, MEM)
            dve.wait_ge(rel_loaded, 16)
            dve.wait_ge(ext_zeroed, 2)
            far = EXT - 257
            nc.vector.tensor_scalar(ext[:, 0:far], ext_zero[:, 0:far], ext[:, far:far + 1], None,
                                    ALU.add).then_inc(ext_ready, 1)
            for k in range(KT):
                add_squares(n_ffn1, sq, acc[:], KT, k)

            def ffn(f, n):
                def tile(F, par, ff, first):
                    dve.wait_ge(f.silu_done, F + 1)
                    dve.wait_ge(f.up_done, 2 * F + 2)
                    if not first:
                        dve.wait_ge(f.lo_done, F - 1)
                    nc.vector.tensor_tensor(prod[:, ff, :], silu[:, ff, :], bank(4 * ff + 2, 2), ALU.mult)\
                        .then_inc(f.prod_done, 1)
                    dve.wait_ge(f.hi_done, F + 1)
                    cut(hid_lo[:, par, ff, :], prod[:, ff, :], hid_hi[:, par, ff, :], f.lo_done)

                def add(down, before, d):
                    dve.wait_ge(f.down_done, down + (d + 1))
                    if before is not None:
                        dve.wait_ge(f.acc_done, before + (d + 1))
                    nc.vector.scalar_tensor_tensor(out=x[:, d, :], in0=bank(2 * (d % 4), 2), scalar=0.5, in1=x[:, d, :],
                                                   op0=ALU.mult, op1=ALU.add).then_inc(f.acc_done, 1)

                for ff in range(2):
                    tile(ff, 0, ff, True)

                def turn(i, first):
                    for r in range(2):
                        for ff in range(2):
                            tile(4 * i + (2 + 2 * r + ff), 1 - r, ff, False)
                        for d in range(KT):
                            add(16 * i + 8 * r, None if first and r == 0 else 16 * i + (8 * r - 8), d)

                turn(0, True)
                with dve.Fori(1, (PAIRS - 1) // 2) as i:
                    turn(i, False)
                last = 8 * (PAIRS - 1)
                for d in range(KT):
                    add(last, last - 8, d)
                    if d >= 1:
                        add_squares(n, sq, acc[:], KT, d - 1)
                add_squares(n, sq, acc[:], KT, KT - 1)

            factors(n_ffn1, diag)
            normalise(n_ffn1, x, nt, C_FFN1, h_lo, h_hi)
            ffn(f1, n_mix)
            factors(n_mix, diag)
            normalise(n_mix, x, nt, C_MIX, h_lo, h_hi)
            dve.wait_ge(kv_hi, 1)
            cut(mk_lo[:], bank(0, 2).rearrange("p (h k) -> p h k", h=MH), mk_hi[:], kv_lo)
            dve.wait_ge(kv_hi, 2)
            cut(mv_lo[:].rearrange("p m (h d) -> p h m d", h=MH), bank(2, 2).rearrange("p (h m d) -> p h m d", h=MH, m=MT),
                mv_hi[:].rearrange("p m (h d) -> p h m d", h=MH), kv_lo)

            def cut_half(t, c):
                which, half = c // 2, c % 2
                a, b = slice(half * HALF, (half + 1) * HALF), t % 2
                dve.wait_ge(qkv_hi, 4 * t + c + 1)
                nc.vector.scalar_tensor_tensor(out=(q_lo, k_lo)[which][b][:, a], in0=bank(half),
                                               scalar=(DH ** -0.5, 1.0)[which],
                                               in1=(q_hi, k_hi)[which][b][:, a].bitcast(F32), op0=ALU.mult,
                                               op1=ALU.subtract).then_inc(qkv_lo, 1)

            def cut_values(t, half):
                dve.wait_ge(v_hi_done, 2 * t + half + 1)
                a = slice(4 * half, 4 * half + 4)
                cut(v_lo[t % 2][:, a, :], bank(7).rearrange("p (c d) -> p c d", c=4), v_hi[t % 2][:, a, :], v_lo_done)

            def mask_bias(h):
                dve.wait_ge(bias_in[h % 2], 16 * (h // 2) + 16)
                nc.vector.memset(bias[0:64, h % 2, BANDK - 64:BANDK], NEG).then_inc(bias_masked, 1)
                nc.vector.memset(bias[64:P, h % 2, 0:64], NEG).then_inc(bias_masked, 1)
                dve.wait_ge(bias_masked, 2 * h + 2)

            def maxima(n):
                w = item(n)[4]
                dve.wait_ge(at_c.qk_done, n + 1)
                nc.vector.tensor_tensor_reduce(pr[n % 2][:, 0:w], ps[:, score_at:score_at + w],
                                               bias[:, n // 8 % 2, BANDK - w:BANDK], -1.0, BIG,
                                               ALU.add, ALU.min, stat[:, 0, n % 2:n % 2 + 1]).then_inc(at_c.max_done, 1)

            def normalise_probs(n):
                w, c = item(n)[4], slice(n % 2, n % 2 + 1)
                dve.wait_ge(at_c.exp_done, n + 1)
                nc.vector.reciprocal(stat[:, 2, c], stat[:, 1, c]).then_inc(at_c.rcp_done, 1)
                dve.wait_ge(at_c.rcp_done, n + 1)
                nc.vector.tensor_scalar(pr[n % 2][:, 0:w], pr[n % 2][:, 0:w], stat[:, 2, c], None,
                                        ALU.mult).then_inc(at_c.norm_done, 1)

            def cut_probs(n):
                w = item(n)[4]
                dve.wait_ge(at_c.pt_hi_done, n + 1)
                cut(pt_lo[:, 0:w], ps[:, turn_at:turn_at + w], pt_hi[:, 0:w], at_c.pt_lo_done)

            def cut_out(n):
                t, b, e, j, w, key = item(n)
                dve.wait_ge(at_c.o_hi_done, n + 1)
                r, a = slice(64 * e, 64 * e + 64), slice(j * P, (j + 1) * P)
                cut(o_lo[r, t, a], item_out[r, :], o_hi[r, t, a], at_c.o_lo_done)

            for c in range(4):
                cut_half(0, c)
            cut_values(0, 0)
            for n in range(N_ITEMS + 1):
                t, m = n // 16, n % 16
                if n < N_ITEMS:
                    if n % 8 == 0:
                        mask_bias(n // 8)
                    maxima(n)
                if n > 0:
                    cut_probs(n - 1)
                if n < N_ITEMS:
                    normalise_probs(n)
                if m == 15 and t < 3:
                    cut_values(t + 1, 0)
                elif n in SECOND_TURNS:
                    cut_values(t, 1)
                if n < N_ITEMS and t < 3:
                    for c in halves_done(n):
                        if c < 4:
                            cut_half(t + 1, c)
                if n > 0:
                    cut_out(n - 1)

            dve.wait_ge(ag_copied, 1)
            nc.vector.memset(conv[:, 1:5, 0:PAD], 0.0).then_inc(pad_done, 1)
            for t in range(CT):
                dve.wait_ge(glu_sig, t + 1)
                v = conv[:, t + 1, PAD:PAD + T]
                if t < 2:
                    a, g = v, (gate[:, 0, :], conv[:, 0, PAD:PAD + T])[t]
                else:
                    a, g = bank(4 * (t - 2), 2), gate[:, 3 - t, :]
                nc.vector.tensor_tensor(v, g, a, ALU.mult).then_inc(glu_v, 1)

            def taps(c, lo, hi):
                for tap in range(lo, hi):
                    src = conv[:, c + 1, tap:tap + T]
                    dst = conv[:, c, PAD:PAD + T]
                    w = params[:, bass.ds(C_DW + TAPS * c + tap, 1)]
                    dve.wait_ge(dw_done, TAPS * c + (tap + 1))
                    if tap == 0:
                        nc.vector.tensor_scalar(dst, src, w, params[:, bass.ds(C_DWB + c, 1)], ALU.mult,
                                                ALU.add).then_inc(dw_done, 1)
                    else:
                        nc.vector.scalar_tensor_tensor(out=dst, in0=src, scalar=w, in1=dst, op0=ALU.mult,
                                                       op1=ALU.add).then_inc(dw_done, 1)

            def mix(g, base, d, s, first):
                dve.wait_ge(g.branch_done, base + s + 1)
                dve.wait_ge(g.sig_done, base + s + 1)
                if first:
                    nc.vector.tensor_tensor(y[:, d, :], gate[:, s, :], bank(2 * s, 2), ALU.mult).then_inc(g.y_done, 1)
                else:
                    nc.vector.tensor_tensor(gate[:, s, :], gate[:, s, :], bank(2 * s, 2), ALU.mult).then_inc(g.mul_done, 1)
                    dve.wait_ge(g.mul_done, base + s + 1)
                    nc.vector.tensor_tensor(y[:, d, :], y[:, d, :], gate[:, s, :], ALU.add).then_inc(g.y_done, 1)

            dve.wait_ge(pad_done, 1)
            dve.wait_ge(glu_v, CT)
            cut_at = (0, 12, 16, 28, TAPS)

            with dve.Fori(0, 2) as i:
                for r in range(2):
                    taps(i, cut_at[2 * r], cut_at[2 * r + 1])
                    mix(g_att, 4 * i + 2 * r, 4 * i + 2 * r, 0, True)
                    taps(i, cut_at[2 * r + 1], cut_at[2 * r + 2])
                    mix(g_att, 4 * i + 2 * r, 4 * i + (2 * r + 1), 1, True)

            def m_query(h):
                for half in range(2):
                    dve.wait_ge(mq_hi_done, 2 * h + half + 1)
                    a = slice(half * HALF, (half + 1) * HALF)
                    nc.vector.scalar_tensor_tensor(out=mq_lo[:, a], in0=bank(half), scalar=P ** -0.5,
                                                   in1=mq_hi[:, a].bitcast(F32), op0=ALU.mult,
                                                   op1=ALU.subtract).then_inc(mq_lo_done, 1)

            def m_max(n):
                c = 2 * (n % 2)
                dve.wait_ge(at_m.qk_done, n + 1)
                nc.vector.tensor_reduce(stat[:, 0, c:c + 2], bank(4 + n % 2).rearrange("p (q k) -> p q k", q=2), AX.X,
                                        ALU.max, negate=True).then_inc(at_m.max_done, 1)

            def m_normalise(n):
                c = 2 * (n % 2)
                dve.wait_ge(at_m.exp_done, n + 1)
                nc.vector.reciprocal(stat[:, 2, c:c + 2], stat[:, 1, c:c + 2]).then_inc(at_m.rcp_done, 1)
                dve.wait_ge(at_m.rcp_done, n + 1)
                for q in range(2):
                    last = nc.vector.tensor_scalar(mp[:, n % 2, q, :], mp[:, n % 2, q, :], stat[:, 2, c + q:c + q + 1],
                                                   None, ALU.mult)
                last.then_inc(at_m.norm_done, 1)

            def m_cut_probs(n):
                dve.wait_ge(at_m.pt_hi_done, n + 1)
                cut(mpt_lo[:], bank(6 + n % 2), mpt_hi[:], at_m.pt_lo_done)

            def m_cut_out(n):
                dve.wait_ge(at_m.o_hi_done, n + 1)
                a = slice((n % 4) * MEM, (n % 4 + 1) * MEM)
                cut(o_lo[:, n // 4, a], bank(2 + n % 2)[:, 0:MEM], o_hi[:, n // 4, a], at_m.o_lo_done)

            m_query(0)
            for n in range(16 + 1):
                if n > 0:
                    m_cut_probs(n - 1)
                if 0 < n < 16 and n % 4 == 0:
                    m_query(n // 4)
                    m_cut_out(n - 1)
                    m_max(n)
                    m_normalise(n)
                else:
                    if n < 16:
                        m_max(n)
                        m_normalise(n)
                    if n > 0:
                        m_cut_out(n - 1)

            def taps_between(lo, hi):
                for n in range(lo, hi):
                    taps(2 + n // TAPS, n % TAPS, n % TAPS + 1)

            for dp in range(3):
                taps_between(21 * dp, min(21 * dp + 16, 2 * TAPS))
                mix(g_mem, 2 * dp, 2 * dp, 0, False)
                taps_between(min(21 * dp + 16, 2 * TAPS), min(21 * dp + 21, 2 * TAPS))
                mix(g_mem, 2 * dp, 2 * dp + 1, 1, False)

            dve.wait_ge(dw_done, CT * TAPS + 1)
            for c in range(1, CT):
                if c >= 2:
                    dve.wait_ge(ln_mean_in, c - 1)
                nc.vector.tensor_tensor(ln_sum, conv[:, 0, PAD:PAD + T] if c == 1 else ln_sum, conv[:, c, PAD:PAD + T],
                                        ALU.add).then_inc(ln_mean_in, 1)
            dve.wait_ge(ln_mean_done, 1)
            for c in range(CT):
                nc.vector.scalar_tensor_tensor(out=conv[:, c, PAD:PAD + T], in0=bank(4, 2), scalar=-1.0 / CONV,
                                               in1=conv[:, c, PAD:PAD + T], op0=ALU.mult, op1=ALU.add).then_inc(ln_centred, 1)
            for c in range(CT):
                add_squares(n_ln, ln_sq, ln_sum, CT, c)
            factors(n_ln, ln_diag)
            mix(g_mem, 6, 6, 0, False)
            dve.wait_ge(*n_ln.past("spread", 1))
            dve.wait_ge(ln_centred, CT)
            for c in range(CT):
                scale(n_ln, conv[:, c, PAD:PAD + T], conv[:, c, PAD:PAD + T], C_LNG + c)
            mix(g_mem, 6, 7, 1, False)
            for c in range(CT):
                dve.wait_ge(*n_ln.past("hi_done", c + 1))
                cut(c_lo[:, c, :], conv[:, c, PAD:PAD + T], c_hi[:, c, :], n_ln.lo_done)

            for dp in range(4):
                for s in range(2):
                    mix(g_conv, 2 * dp, 2 * dp + s, s, False)

            for k in range(KT):
                dve.wait_ge(y_hi_done, k + 1)
                cut(y_lo[:, k, :], y[:, k, :], y_hi[:, k, :], y_lo_done)
            for k in range(KT):
                dve.wait_ge(out_done, k + 1)
                dve.wait_ge(x_back[k], 16)
                nc.vector.tensor_tensor(x[:, k, :], x[:, k, :], bank(2 * (k % 4), 2), ALU.add).then_inc(x_added, 1)
                if k >= 1:
                    add_squares(n_ffn2, sq, acc[:], KT, k - 1)
            add_squares(n_ffn2, sq, acc[:], KT, KT - 1)

            factors(n_ffn2, diag)
            normalise(n_ffn2, x, nt, C_FFN2, h_lo, h_hi)
            ffn(f2, n_fin)
            factors(n_fin, diag)
            dve.wait_ge(*n_fin.past("spread", 1))
            for k in range(KT):
                scale(n_fin, x[:, k, :], x[:, k, :], C_FINAL + k)


def stream(inputs):
    import numpy as np

    def cut(w, rows, width):
        w = np.asarray(w)
        r, c = w.shape
        b = w.reshape(r // rows, rows // P, P, c // width, width)
        return b.transpose(0, 3, 2, 1, 4).reshape(r // rows, c // width, P, rows // P * width)

    units = []

    def ffn(up, down):
        up, down = cut(up[0], D, P)[0], cut(down[0], 2 * P, 4 * P)
        tiles = D_FF // P
        for g in range(PAIRS + 1):
            if g < PAIRS:
                for f in (2 * g, 2 * g + 1):
                    units.extend([up[f], up[tiles + f]])
            if g > 0:
                units.extend(down[g - 1])

    w_in = cut(inputs["w_in"][0], D, P)[0]
    a0, m0, g0 = 2 * CT, 2 * CT + 12, 2 * CT + 16

    def branch(b, w):
        w = cut(w[0], CONV, 2 * P)[0]
        for dp in range(KT // 2):
            units.extend([w_in[g0 + KT * b + 2 * dp], w_in[g0 + KT * b + 2 * dp + 1], w[dp]])

    ffn(inputs["ffn1_w_up"], inputs["ffn1_w_down"])
    units.extend(cut(inputs["mem_w_kv"][0], D, P)[0])
    for t in range(4):
        units.extend([w_in[a0 + t], w_in[a0 + 4 + t], w_in[a0 + 8 + t]])
    for t in range(CT):
        units.extend([w_in[t], w_in[CT + t]])
    branch(1, inputs["att_w_o"])
    units.extend(w_in[m0:m0 + MH])
    branch(2, inputs["mem_w_o"])
    branch(0, inputs["conv_w_pw"])
    units.extend(cut(inputs["w_out"][0], D, P)[0])
    ffn(inputs["ffn2_w_up"], inputs["ffn2_w_down"])
    assert len(units) == UNITS
    return np.stack(units)


def kernel(**inputs):
    import numpy as np
    import concourse.bacc as bacc
    from concourse.bass_utils import run_bass_kernel_spmd

    inputs = {k: np.asarray(v) for k, v in inputs.items()}

    def columns(v):
        return v.reshape(-1, P).T

    params = np.concatenate(
        [columns(inputs[n].reshape(-1)) for n in ("ffn1_norm", "mix_norm", "mem_norm", "ffn2_norm", "final_norm", "b_gate")]
        + [inputs["conv_dw_w"][0].reshape(TAPS, CT, P).transpose(2, 1, 0).reshape(P, CT * TAPS)]
        + [columns(inputs[n][0]) for n in ("conv_dw_b", "conv_ln_g", "conv_ln_b")], axis=1)
    arrays = {
        "x_in": np.ascontiguousarray(inputs["x"][0].T).reshape(KT, P, T),
        "mem_in": np.ascontiguousarray(inputs["mem"][0].reshape(MEM, KT, P).transpose(2, 1, 0)),
        "weights": stream(inputs),
        "params": np.ascontiguousarray(params),
        "rel_bias": np.ascontiguousarray(inputs["att_rel_bias"][0][:, ::-1]),
    }
    nc = bacc.Bacc("TRN2", target_bir_lowering=False, num_devices=1)
    args = [nc.dram_tensor(n, a.shape, F32, kind="ExternalInput").ap() for n, a in arrays.items()]
    out = nc.dram_tensor("y_out", (KT, P, T), F32, kind="ExternalOutput").ap()
    program(nc, *args, out)
    r = run_bass_kernel_spmd(nc, [arrays], core_ids=[0])
    return np.ascontiguousarray(r.results[0]["y_out"].reshape(D, T).T)[None]
```

```python
from contextlib import ExitStack

import concourse.bass as bass
from concourse import mybir

F32 = mybir.dt.float32
F32R = mybir.dt.float32r
ALU = mybir.AluOpType
ACT = mybir.ActivationFunctionType
AX = mybir.AxisListType

P = 128
T = 1024
HALF = 512
D = 1024
KT = D // P
D_FF = 2816
PAIRS = D_FF // (2 * P)
CONV = 512
CT = CONV // P
TAPS = 31
PAD = TAPS - 1
MEM = 256
MT = MEM // P
HEADS = 8
DH = 64
REL = 192
BANDK = 640
EXT = 768
FAR = EXT - 257
MH = 4
EPS = 1e-6
NEG = -1e30
BIG = 3.0e38

U_FFN1 = 0
U_QKV = U_FFN1 + 6 * PAIRS
U_CONV = U_QKV + 3 * 4 + 2 * MH
U_ATT = U_CONV + 2 * CT
U_MQ = U_ATT + 12
U_MEMO = U_MQ + MH
U_CONVO = U_MEMO + 12
U_OUT = U_CONVO + 12
U_FFN2 = U_OUT + KT
UNITS = U_FFN2 + 6 * PAIRS

C_FFN1, C_MIX, C_MEM, C_FFN2, C_FINAL = 0, 8, 16, 24, 32
C_GATE = 40
C_DW = C_GATE + 24
C_DWB = C_DW + CT * TAPS
C_LNG = C_DWB + CT
C_LNB = C_LNG + CT
N_PAR = C_LNB + CT


def program(nc, x_in, mem_in, weights, params_in, rel_in, y_out):
    rel_ext = nc.dram_tensor("rel_ext", (HEADS, EXT), F32, kind="Internal")
    bias_rows = nc.dram_tensor("bias_rows", (HEADS, P, BANDK), F32, kind="Internal").ap()
    x_spill = nc.dram_tensor("x_spill", (KT, P, T), F32, kind="Internal").ap()

    with ExitStack() as ctx:
        def sem(name):
            return ctx.enter_context(nc.semaphore(name))

        at = [(nc.sbuf_base + 31) // 32 * 32]

        def place(name, shape, dt, offset):
            return nc.alloc_sbuf_tensor_at(name, shape, dt, offset=offset)

        def fixed(name, shape, dt=F32):
            n = 4
            for s in shape[1:]:
                n *= s
            o = at[0]
            at[0] += (n + 31) // 32 * 32
            return place(name, shape, dt, o)

        K = 1024
        params = fixed("params", [P, N_PAR])
        ones = fixed("ones", [P, P])
        ident = fixed("ident", [P, P])
        zero = fixed("zero", [P, 1])
        eps = fixed("eps", [P, 1])
        cols = fixed("cols", [P, 2, 8])
        spare = fixed("spare", [P, 4])
        stat = fixed("stat", [P, 3, 8])
        w_raw = fixed("w_raw", [P, 2, T])
        w_hi = fixed("w_hi", [P, 2, T], F32R)
        w_lo = fixed("w_lo", [P, 2, T], F32R)
        h_hi = fixed("h_hi", [P, KT, T], F32R)
        h_lo = fixed("h_lo", [P, KT, T], F32R)
        X = at[0]
        A = X + 32 * K
        x = place("x", [P, KT, T], F32, X)
        hid_hi = place("hid_hi", [P, 2, 2, T], F32R, A)
        hid_lo = place("hid_lo", [P, 2, 2, T], F32R, A + 16 * K)
        silu = place("silu", [P, 2, T], F32, A + 32 * K)
        prod = place("prod", [P, 2, T], F32, A + 40 * K)
        sq = place("sq", [P, 4, HALF], F32, A + 32 * K)
        diag = place("diag", [P, T], F32, A + 48 * K)
        acc = place("acc", [P, T], F32, A + 56 * K)
        nt = place("nt", [P, 4, HALF], F32, A + 60 * K)
        M = A + 68 * K + 1536
        assert M + 16 * K <= nc.sbuf_usable_end
        mk_hi = place("mk_hi", [P, MH, MEM], F32R, M)
        mk_lo = place("mk_lo", [P, MH, MEM], F32R, M + 4 * K)
        mv_hi = place("mv_hi", [P, MT, MH * P], F32R, M + 8 * K)
        mv_lo = place("mv_lo", [P, MT, MH * P], F32R, M + 12 * K)
        mem_hi = place("mem_hi", [P, KT, MEM], F32R, M)
        mem_lo = place("mem_lo", [P, KT, MEM], F32R, M + 8 * K)
        mem_kept = [place("mem_kept_hi", [P, KT, MEM], F32R, A + 8 * K),
                    place("mem_kept_lo", [P, KT, MEM], F32R, A + 24 * K)]
        mem = place("mem", [P, KT, MEM], F32, A + 60 * K)
        msq = place("msq", [P, 2, MEM], F32, A + 52 * K)
        mdiag = place("mdiag", [P, MEM], F32, A + 54 * K)
        macc = place("macc", [P, MEM], F32, A + 55 * K)
        ext = place("ext", [HEADS, EXT], F32, A + 24 * K)
        mspread = place("mspread", [P, MEM], F32, A + 27 * K)
        mnt = place("mnt", [P, 2, MEM], F32, A + 28 * K)
        ext_zero = place("ext_zero", [HEADS, FAR], F32, A + 30 * K)
        S0, S1 = X + 8 * K, A + 32 * K

        def both(name, shape, offset):
            return [place(f"{name}{n}", shape, F32R, s + offset * K) for n, s in enumerate((S0, S1))]

        q_hi, q_lo = both("q_hi", [P, T], 0), both("q_lo", [P, T], 4)
        k_hi, k_lo = both("k_hi", [P, T], 8), both("k_lo", [P, T], 12)
        v_hi, v_lo = both("v_hi", [P, KT, P], 16), both("v_lo", [P, KT, P], 20)
        vT = place("vT", [P, 4, T], F32, A)
        o_hi = place("o_hi", [P, 4, T], F32R, A)
        o_lo = place("o_lo", [P, 4, T], F32R, A + 16 * K)
        bias = place("bias", [P, 2, BANDK], F32, A + 56 * K)
        blank = place("blank", [P, P], F32, A + 68 * K + 512)
        pt_hi = place("pt_hi", [P, 5, 2, P], F32R, A + 61 * K)
        pt_lo = place("pt_lo", [P, 5, 2, P], F32R, X)
        pr = [place("pr0", [P, BANDK], F32, X + 5 * K), place("pr1", [P, BANDK], F32, A + 66 * K)]
        gate = place("gate", [P, 2, T], F32, X)
        y = place("y", [P, KT, T], F32, A + 32 * K)
        SEG = PAD + T + 2
        conv = place("conv", [P, 5, SEG], F32, X + 32 * K - 5 * SEG * 4)
        c_hi = place("c_hi", [P, CT, T], F32R, A)
        c_lo = place("c_lo", [P, CT, T], F32R, A + 16 * K)
        mq_hi = place("mq_hi", [P, T], F32R, X)
        mq_lo = place("mq_lo", [P, T], F32R, X + 4 * K)
        mp = place("mp", [P, 2, 2, MEM], F32, A + 64 * K)
        c2 = X + 32 * K - 3 * SEG * 4
        mpt_hi = place("mpt_hi", [P, 2 * MEM], F32R, c2)
        mpt_lo = place("mpt_lo", [P, 2 * MEM], F32R, c2 + 2 * K)
        y_hi = place("y_hi", [P, KT, T], F32R, X - 64 * K)
        y_lo = place("y_lo", [P, KT, T], F32R, X - 32 * K)

        ln_sum = conv[:, 4, PAD:PAD + T]
        ln_sq = place("ln_sq", [P, 2, T], F32, M)
        ln_diag = place("ln_diag", [P, T], F32, M + 8 * K)

        ps = ctx.enter_context(nc.psum_tensor("ps", [P, 8 * HALF], F32))

        def bank(b, n=1):
            return ps[:, b * HALF:(b + n) * HALF]

        w_loaded = [sem("w_loaded0"), sem("w_loaded1")]
        w_rounded = sem("w_rounded")
        w_split = sem("w_split")
        w_used = sem("w_used")
        params_loaded = sem("params_loaded")
        rel_loaded = sem("rel_loaded")
        ext_stored = sem("ext_stored")
        rows_stored = sem("rows_stored")
        mem_loaded = sem("mem_loaded")
        x_loaded = [[sem(f"x_loaded{half}_{k}") for k in range(KT // 2)] for half in range(2)]
        const_ready = sem("const_ready")
        ext_zeroed = sem("ext_zeroed")
        ident_ready = sem("ident_ready")
        ext_ready = sem("ext_ready")
        x_spilled = sem("x_spilled")
        x_back = [sem(f"x_back{k}") for k in range(KT)]
        y_stored = sem("y_stored")

        class Norm:

            def __init__(self, sems, index, order, steps=None):
                self.sems, self.index, self.order, self.steps = sems, index, order, steps or {}
                self.halves = 1 + max(h for h, _ in order)
                self.squared, self.summed = sems["squared"], sems["summed"]
                self.cols_done = sems["cols_done"]
                self.std_done = sems["std_done"]
                self.rstd_done = sems["rstd_done"]
                self.diag_done = sems["diag_done"]
                self.spread = sems["spread"]
                self.scaled = sems["scaled"]
                self.hi_done = sems["hi_done"]
                self.lo_done = sems["lo_done"]

            def past(self, name, count):
                each = {"squared": KT, "summed": KT - 1, "scaled": KT, "hi_done": KT, "lo_done": KT}.get(name, 1)
                return self.sems[name], self.index * self.halves * each + count

            def sums(self, n):
                h, k = self.order[n]
                n = self.order.index((h, max(k, 1)))
                return sum(1 for _, k in self.order[:n + 1] if k > 0)

            def sums_of(self, h):
                return self.sums(max(n for n, (a, _) in enumerate(self.order) if a == h))

        def norm_sems(name):
            return {s: sem(f"{name}_{s}") for s in ("squared", "summed", "cols_done", "std_done", "rstd_done",
                                                    "diag_done", "spread", "scaled", "hi_done", "lo_done")}

        class Ffn:
            def __init__(self, name, unit):
                self.unit = unit
                self.up_done = sem(f"{name}_up_done")
                self.silu_done = sem(f"{name}_silu_done")
                self.prod_done = sem(f"{name}_prod_done")
                self.hi_done = sem(f"{name}_hi_done")
                self.lo_done = sem(f"{name}_lo_done")
                self.down_done = sem(f"{name}_down_done")
                self.acc_done = sem(f"{name}_acc_done")

        class Gated:
            def __init__(self, name, unit):
                self.unit = unit
                self.gate_done = sem(f"{name}_gate_done")
                self.sig_done = sem(f"{name}_sig_done")
                self.branch_done = sem(f"{name}_branch_done")
                self.y_done = sem(f"{name}_y_done")
                self.mul_done = sem(f"{name}_mul_done")

        of_x = norm_sems("norm")
        by_tile = [(h, k) for k in range(KT) for h in range(2)]
        by_half = [(h, k) for h in range(2) for k in range(KT)]
        n_ffn1 = Norm(of_x, 0, by_half, {KT + 4: (0, 1), KT + 5: (2,), KT + 6: (3, 4), KT + 7: (5,)})
        n_mix = Norm(of_x, 1, by_half, {KT + 4: (0, 1), KT + 5: (2,), KT + 6: (3, 4), KT + 7: (5,)})
        n_ffn2, n_fin = Norm(of_x, 2, by_tile[:2 * KT - 4] + [(0, 6), (0, 7), (1, 6), (1, 7)]), Norm(of_x, 3, by_half)
        of_others = norm_sems("other_norm")
        n_mem = Norm(of_others, 0, [(0, k) for k in range(KT)])
        n_ln = Norm(of_others, 1, [(0, k) for k in range(CT)])
        FACTORS_AT = KT + 1
        mem_spread_kept, mem_moved = sem("mem_spread_kept"), sem("mem_moved")
        f1, f2 = Ffn("f1", U_FFN1), Ffn("f2", U_FFN2)
        g_att, g_mem, g_conv = Gated("gatt", U_ATT), Gated("gmem", U_MEMO), Gated("gconv", U_CONVO)
        kv_done, kv_hi, kv_lo = sem("kv_done"), sem("kv_hi"), sem("kv_lo")
        qkv_done, qkv_hi, qkv_lo = sem("qkv_done"), sem("qkv_hi"), sem("qkv_lo")
        vt_copied, vt_turned, v_hi_done, v_lo_done = sem("vt_copied"), sem("vt_turned"), sem("v_hi_done"), sem("v_lo_done")
        bias_in, bias_masked = [sem("bias_in0"), sem("bias_in1")], sem("bias_masked")
        ag_done, ag_copied = sem("ag_done"), sem("ag_copied")

        class Att:
            def __init__(self, name):
                self.qk_done = sem(f"{name}_qk_done")
                self.max_done = sem(f"{name}_max_done")
                self.exp_done = sem(f"{name}_exp_done")
                self.rcp_done = sem(f"{name}_rcp_done")
                self.norm_done = sem(f"{name}_norm_done")
                self.turned = sem(f"{name}_turned")
                self.pt_hi_done = sem(f"{name}_pt_hi_done")
                self.pt_lo_done = sem(f"{name}_pt_lo_done")
                self.pv_done = sem(f"{name}_pv_done")
                self.o_hi_done = sem(f"{name}_o_hi_done")
                self.o_lo_done = sem(f"{name}_o_lo_done")

        at_c, at_m = Att("catt"), Att("matt")
        mq_done, mq_hi_done, mq_lo_done = sem("mq_done"), sem("mq_hi_done"), sem("mq_lo_done")
        glu_done, glu_sig, glu_v, pad_done = sem("glu_done"), sem("glu_sig"), sem("glu_v"), sem("pad_done")
        dw_done = sem("dw_done")
        ln_mean_in, ln_mean_done = sem("nln_mean_in"), sem("nln_mean_done")
        ln_centred, ln_silu_done = sem("nln_centred"), sem("nln_silu_done")
        y_hi_done, y_lo_done = sem("y_hi_done"), sem("y_lo_done")
        out_done, x_added = sem("out_done"), sem("x_added")

        def key_width(j):
            return min(j + 1, 5) * P

        N_ITEMS = 64
        SECOND_TURNS = (0, 17, 33, 49)
        turn_at = 4 * HALF
        pair_out = bank(6)[:, 0:2 * P]


        def item(n):
            t, m = n // 16, n % 16
            j = m % 8
            return t, t % 2, m // 8, j, key_width(j), max(j - 4, 0) * P

        def fill(n):
            t, m = n // 16, n % 16
            if t < 3:
                first = U_QKV + (3, 10, 17)[t]
                kinds = ("q", "k", "v") if t == 2 else ("q", "mem", "mem", "k", "mem", "mem", "v")
            else:
                first, kinds = U_CONV, ("a0", "g0", "a1", "g1")
            parts = []
            for i, kind in enumerate(kinds):
                count = 4 if kind == "mem" else 2 * KT
                parts += [(kind, first + i, p, count) for p in range(count)]
            each = len(parts) // 16
            return parts[each * m:each * (m + 1)]

        def halves_done(n):
            return [(kind, p // 8) for kind, _, p, _ in fill(n) if kind != "mem" and p % 8 == 7]

        def memory_done(n):
            done = [mem_unit(u) for kind, u, p, count in fill(n) if kind == "mem" and p == count - 1]
            return [c if c < MH else c // 2 + 2 for c in done if c < MH or c % 2 == 1]

        def mem_unit(u):
            return (1, 2, 4, 5, 8, 9, 11, 12).index(u - (U_QKV + 3))

        block = ctx.enter_context(nc.Block())

        def load_x(engine, half):
            a = slice(half * HALF, (half + 1) * HALF)
            for k in range(0, KT, 2):
                engine.dma_start(x[:, k:k + 2, a], x_in[k:k + 2, :, a].rearrange("k p t -> p k t"))\
                    .then_inc(x_loaded[half][k // 2], 16)

        @block.sync
        def _(sp):
            load_x(sp, 0)
            for s in range(2):
                sp.dma_start(w_raw[:, s, :], weights[s]).then_inc(w_loaded[s], 16)
            with sp.Fori(1, UNITS // 2) as i:
                for s in range(2):
                    sp.wait_ge(w_split, 2 * i + (s - 1))
                    sp.dma_start(w_raw[:, s, :], weights[2 * i + s]).then_inc(w_loaded[s], 16)
            for half in range(2):
                for k in range(KT):
                    a = slice(half * HALF, (half + 1) * HALF)
                    sp.wait_ge(*n_fin.past("scaled", half * KT + k + 1))
                    sp.dma_start(y_out[k][:, a], x[:, k, a]).then_inc(y_stored, 16)
            sp.wait_ge(y_stored, 2 * KT * 16)

        @block.gpsimd
        def _(pool):
            nc.gpsimd.memset(zero[:], 0.0).then_inc(const_ready, 1)
            nc.gpsimd.memset(eps[:], EPS).then_inc(const_ready, 1)
            nc.gpsimd.memset(ones[:], 1.0).then_inc(const_ready, 1)
            nc.gpsimd.memset(ident[:], 0.0).then_inc(const_ready, 1)
            nc.gpsimd.memset(blank[:], 0.0).then_inc(const_ready, 1)
            pool.wait_ge(const_ready, 5)
            nc.gpsimd.affine_select(out=ident[:], in_=ident[:], compare_op=ALU.not_equal, fill=1.0, base=0,
                                    pattern=[[-1, P]], channel_multiplier=1).then_inc(ident_ready, 1)

            def cut(s, loaded, rounded):
                pool.wait_ge(w_loaded[s], loaded)
                nc.gpsimd.tensor_tensor(w_hi[:, s, :], w_raw[:, s, :], zero[:].to_broadcast([P, T]),
                                        ALU.add).then_inc(w_rounded, 1)
                pool.wait_ge(w_rounded, rounded)
                nc.gpsimd.tensor_tensor(w_lo[:, s, :], w_raw[:, s, :], w_hi[:, s, :].bitcast(F32),
                                        ALU.subtract).then_inc(w_split, 1)

            for s in range(2):
                cut(s, 16, s + 1)
            with pool.Fori(1, UNITS // 2) as i:
                for s in range(2):
                    pool.wait_ge(w_used, 2 * i + (s - 1))
                    cut(s, 16 * i + 16, 2 * i + (s + 1))

        @block.tensor
        def _(pe):
            release = [False]

            def unit(u, first=False):
                pe.wait_ge(w_split, u + 1)
                release[0] = not first
                return u % 2 if isinstance(u, int) else None

            def step(out, stationary, moving, start, stop):
                (sh, sl), (mh, ml) = stationary, moving
                mm = nc.tensor.matmul(out, sh, mh, start=start, stop=False)
                if release[0]:
                    mm.then_inc(w_used, 1)
                    release[0] = False
                nc.tensor.matmul(out, sh, ml, start=False, stop=False)
                return nc.tensor.matmul(out, sl, mh, start=False, stop=stop)

            def weight(slot, at_col):
                return w_hi[:, slot, at_col:at_col + P], w_lo[:, slot, at_col:at_col + P]

            def dense(outs, slot, src, ks, done, off=0, width=P, hook=None):
                for half, out in enumerate(outs):
                    if out is None:
                        continue
                    for n, k in enumerate(ks):
                        if hook is not None:
                            hook(k)
                        mm = step(out, weight(slot, off + n * width), src(k, half), n == 0, n == len(ks) - 1)
                if done is not None:
                    mm.then_inc(done, 1)

            def dense_two(u, outs, src, done, count, before):
                for half in range(2):
                    lag = (4, KT)[half]
                    for n in range(KT + lag):
                        if n < KT:
                            before(half, n)
                        for slot, k in ((0, n), (1, n - lag)):
                            if not 0 <= k < KT:
                                continue
                            if slot == 1 and k == 0 and half == 0:
                                pe.wait_ge(w_split, u + 2)
                            if slot == 1 and n == KT and half == 1:
                                release[0] = True
                            mm = step(outs[slot][half], weight(slot, k * P), src(k, half), k == 0, k == KT - 1)
                            if half == 1 and k == KT - 1:
                                mm.then_inc(done, count)

            def rows(hi, lo):
                def src(k, half):
                    a = slice(half * HALF, (half + 1) * HALF)
                    return hi[:, k, a], lo[:, k, a]
                return src

            def pair(slot):
                return [bank(2 * slot), bank(2 * slot + 1)]

            def norm_cols(n, a, half=0, width=HALF, b=None):
                pe.wait_ge(*n.past("summed", n.sums_of(half)))
                out = bank(4 + half if b is None else b)
                for i in range(width // P):
                    mm = nc.tensor.matmul(out[:, i:i + 1], a[:, half * HALF + i * P:half * HALF + (i + 1) * P],
                                          ones[:, 0:1], start=True, stop=True)
                    if release[0]:
                        mm.then_inc(w_used, 1)
                        release[0] = False
                mm.then_inc(n.cols_done, 1)

            def norm_spread(n, dg, half=0, width=HALF, at_col=None):
                pe.wait_ge(*n.past("diag_done", half + 1))
                at_col = (6 + half) * HALF if at_col is None else at_col
                for a in range(0, width, HALF):
                    w, at_tok = min(HALF, width - a), half * HALF + a
                    mm = nc.tensor.matmul(ps[:, at_col + a:at_col + a + w], ones[:], dg[:, at_tok:at_tok + w],
                                          start=True, stop=True)
                mm.then_inc(n.spread, 1)

            pe.wait_ge(const_ready, 5)

            def memory_part(u, p):
                c, slot = mem_unit(u), u % 2
                hi, lo = mem_kept
                if p == 0:
                    unit(u)
                    if c == 0:
                        pe.wait_ge(mem_moved, 32)
                    if c % 4 == 0:
                        pe.wait_ge(v_lo_done, 2 + c // 2)
                    if 0 < c <= MH or c == 6:
                        pe.wait_ge(kv_lo, min(c, 5))
                if c < MH:
                    for k in (2 * p, 2 * p + 1):
                        mm = step(bank(7)[:, 0:MEM], weight(slot, k * P), (hi[:, k, :], lo[:, k, :]), k == 0, k == KT - 1)
                    if p == 3:
                        mm.then_inc(kv_done, 1)
                else:
                    if p == 0 and c % 2 == 0:
                        nc.tensor.matmul(bank(7), blank[:], blank[:, None, :].to_broadcast([P, 4, P]),
                                         start=True, stop=False)
                    k, w = 4 * (c % 2) + p, slice(2 * P * p, 2 * P * (p + 1))
                    for m in range(MT):
                        a = slice(m * P, (m + 1) * P)
                        mm = step(bank(7)[:, m * 2 * P:(m + 1) * 2 * P], (hi[:, k, a], lo[:, k, a]),
                                  (w_hi[:, slot, w], w_lo[:, slot, w]), False, k == KT - 1 and m == MT - 1)
                    if k == KT - 1:
                        mm.then_inc(kv_done, 1)

            def after_sums(n, bank_free):
                def before(half, k):
                    bank_free(half, k)
                    if half == 0 and k == 4:
                        norm_cols(n, acc, 1)
                    if half == 0 and k == 6:
                        norm_spread(n, diag, 1)
                    pe.wait_ge(*n.past("lo_done", half * KT + k + 1))
                return before

            def ffn(f, n, n_next, before):
                def up(base, slot_free):
                    for s in range(4):
                        slot = unit_in(base, s)
                        pe.wait_ge(*slot_free(s))
                        dense(pair(s), slot, rows(h_hi, h_lo), range(KT), f.up_done)

                def down(base, par, slot_free):
                    for d in range(KT):
                        if d % 4 == 0:
                            slot = unit_in(base, d // 4)
                        pe.wait_ge(*slot_free(d))
                        dense(pair(d % 4), slot, rows(hid_hi[:, par], hid_lo[:, par]), range(2), f.down_done,
                              off=(d % 4) * P, width=4 * P)

                def unit_in(base, s):
                    unit(base + s)
                    return s % 2

                def turn(i, first):
                    for r in range(2):
                        base = f.unit + 4 + 12 * i + 6 * r
                        if first and r == 0:
                            up(base, lambda s: (f.prod_done, s // 2 + 1))
                        else:
                            up(base, lambda s: (f.acc_done, 16 * i + (8 * r - 3 + s)))
                        pe.wait_ge(f.lo_done, 4 * i + (2 * r + 2))
                        down(base + 4, r, lambda d: (f.prod_done, 4 * i + (2 * r + 3 + d // 2)) if d < 4
                             else (f.acc_done, 16 * i + (8 * r + d - 3)))

                unit(f.unit, first=(f is f1))
                dense_two(f.unit, (pair(0), pair(1)), rows(h_hi, h_lo), f.up_done, 1, before)
                for s in range(2, 4):
                    slot = unit_in(f.unit, s)
                    if f is f1 and s == 3:
                        norm_cols(n_mem, macc, 0, MEM, b=7)
                        dense(pair(3)[0:1], slot, rows(h_hi, h_lo), range(KT), None)
                        norm_spread(n_mem, mdiag, 0, MEM, at_col=7 * HALF)
                        pe.wait_ge(mem_spread_kept, 1)
                        dense([None, bank(7)], slot, rows(h_hi, h_lo), range(KT), f.up_done)
                    else:
                        if s == 3:
                            pe.wait_ge(*n.past("lo_done", 2 * KT))
                        dense(pair(s), slot, rows(h_hi, h_lo), range(KT), f.up_done)
                turn(0, True)
                with pe.Fori(1, (PAIRS - 1) // 2) as i:
                    turn(i, False)
                pe.wait_ge(f.lo_done, 2 * PAIRS)
                last, u, par = 8 * (PAIRS - 1), f.unit + 6 * PAIRS - 2, (PAIRS - 1) % 2
                for half in range(2):
                    for d in range(KT):
                        slot = (u + d // 4) % 2
                        if half == 0:
                            if d % 4 == 0:
                                unit(u + d // 4, first=(d == 4))
                            pe.wait_ge(f.acc_done, last - 3 + d // 2)
                            b = d
                        else:
                            if d == 4:
                                release[0] = True
                            pe.wait_ge(f.acc_done, last + (d + 1 if d < 4 else KT + d - 3))
                            b = d % 4
                        outs = [None, None]
                        outs[half] = bank(b)
                        dense(outs, slot, rows(hid_hi[:, par], hid_lo[:, par]), range(2), f.down_done,
                              off=(d % 4) * P, width=4 * P)
                        if (half, d) == (1, 1):
                            norm_cols(n_next, acc, 0)
                        if (half, d) == (1, 3):
                            norm_spread(n_next, diag, 0)

            norm_cols(n_ffn1, acc, 0)
            norm_spread(n_ffn1, diag, 0)
            ffn(f1, n_ffn1, n_mix, after_sums(n_ffn1, lambda half, k: None))

            def project(t, kind, u, p):
                c, half, k = "qkv".index(kind), p // 8, p % 8
                if p == 0:
                    unit(u)
                if k == 0:
                    if c > 0:
                        pe.wait_ge(qkv_lo, 4 * t + 2 * c - 1 + half)
                    else:
                        pe.wait_ge(vt_copied, 2 * t - 1 + half)
                mm = step(bank(half), weight(u % 2, k * P), rows(h_hi, h_lo)(k, half), k == 0, k == KT - 1)
                if k == KT - 1:
                    mm.then_inc(qkv_done, 1)

            def conv_part(c, u, p):
                half, k = p // 8, p % 8
                if p == 0:
                    unit(u)
                if k == 0:
                    if c > 0:
                        pe.wait_ge(ag_copied, 2 * c - 1 + half)
                    else:
                        pe.wait_ge(vt_copied, 7 + half)
                mm = step(bank(half), weight(u % 2, k * P), rows(h_hi, h_lo)(k, half), k == 0, k == KT - 1)
                if k == KT - 1:
                    mm.then_inc(ag_done, 1)

            def turn_values(t, half):
                pe.wait_ge(vt_copied, 2 * t + half + 1)
                if 2 * t + half > 0:
                    pe.wait_ge(v_lo_done, 2 * t + half)
                    if half == 0:
                        pe.wait_ge(kv_lo, (0, 4, 6, 6)[t])
                for i in range(4):
                    c = 4 * half + i
                    mm = nc.tensor.transpose(bank(7)[:, i * P:(i + 1) * P], vT[:, t, c * P:(c + 1) * P], ident[:])
                mm.then_inc(vt_turned, 1)

            def scores(n):
                t, b, e, j, w, key = item(n)
                if n % 16 == 0:
                    pe.wait_ge(qkv_lo, 4 * t + 4)
                if n > 0:
                    pe.wait_ge(at_c.max_done, n)
                r, qs = slice(64 * e, 64 * e + 64), slice(j * P, (j + 1) * P)
                size = w if w <= HALF else w // 2
                for i in range(w // size):
                    ks = slice(key + i * size, key + (i + 1) * size)
                    mm = step(bank(2 + i)[:, 0:size], (q_hi[b][r, qs], q_lo[b][r, qs]),
                              (k_hi[b][r, ks], k_lo[b][r, ks]), True, True)
                mm.then_inc(at_c.qk_done, 1)

            def turn_probs(n):
                w = item(n)[4]
                pe.wait_ge(at_c.norm_done, n + 1)
                if n > 0:
                    pe.wait_ge(at_c.pt_lo_done, n)
                for i in range(w // P):
                    to = turn_at + w - (i + 1) * P
                    mm = nc.tensor.transpose(ps[:, to:to + P], pr[n % 2][:, i * P:(i + 1) * P], ident[:])
                mm.then_inc(at_c.turned, 1)

            def values(n):
                t, b, e, j, w, key = item(n)
                pe.wait_ge(at_c.pt_lo_done, n + 1)
                if n % 8 == 1:
                    pe.wait_ge(v_lo_done, 2 * t + 2)
                if n > 1:
                    pe.wait_ge(at_c.o_lo_done, n // 2)
                hi, lo = [p.rearrange("p c q k -> p (c q k)") for p in (pt_hi, pt_lo)]
                even, odd = key_width(j - 1) // P, w // P
                both_see = [s for s in range(1, even + 1) if s < odd]
                order = both_see + [0] + list(range(len(both_see) + 1, even + 1))
                for s in order:
                    first, last = (2 * s - 1) * P if s > 0 else 0, (2 * s + 1) * P if s < odd else 2 * s * P
                    out = pair_out[:, P if s == 0 else 0:2 * P if s < odd else P]
                    mm = step(out, (v_hi[b][:, j - s, :], v_lo[b][:, j - s, :]), (hi[:, first:last], lo[:, first:last]),
                              s == order[0], s == order[-1])
                mm.then_inc(at_c.pv_done, 1)

            unit(U_QKV)

            def sums_have_left(half, k):
                d = {(0, 0): 4, (0, 4): 6, (1, 0): 7}.get((half, k))
                if d is not None:
                    pe.wait_ge(f1.acc_done, 8 * (PAIRS - 1) + KT + d + 1)

            dense_two(U_QKV, (pair(0), pair(1)), rows(h_hi, h_lo), qkv_done, 2, after_sums(n_mix, sums_have_left))
            slot = unit(U_QKV + 2)
            for half in range(2):
                pe.wait_ge(qkv_lo, half + 1)
                outs = [None, None]
                outs[half] = bank(half)
                dense(outs, slot, rows(h_hi, h_lo), range(KT), qkv_done)
            turn_values(0, 0)
            for n in range(N_ITEMS + 1):
                t, m = n // 16, n % 16
                if n < N_ITEMS:
                    scores(n)
                if n > 0:
                    turn_probs(n - 1)
                if m == 15:
                    if t < 3:
                        turn_values(t + 1, 0)
                elif n in SECOND_TURNS:
                    turn_values(t, 1)
                if n < N_ITEMS:
                    for kind, u, p, _ in fill(n):
                        if kind == "mem":
                            memory_part(u, p)
                        elif t < 3:
                            project(t + 1, kind, u, p)
                        else:
                            conv_part(u - U_CONV, u, p)
                if n > 0 and n % 2 == 0:
                    values(n - 1)

            for c in range(4):
                slot = unit(U_CONV + 4 + c)
                if c == 0:
                    pe.wait_ge(ag_copied, 8)
                elif c == 1:
                    pe.wait_ge(at_c.max_done, N_ITEMS)
                elif c == 2:
                    pe.wait_ge(at_c.pt_lo_done, N_ITEMS)
                else:
                    pe.wait_ge(at_c.o_lo_done, N_ITEMS // 2)
                dense(pair(c), slot, rows(h_hi, h_lo), range(KT), glu_done)

            def gates(g, base, u, s, slot):
                unit(u)
                pe.wait_ge(g.y_done, base + s + 1)
                dense(pair(s), slot, rows(h_hi, h_lo), range(KT), g.gate_done)

            def branch(g, base, s, slot, src):
                pe.wait_ge(g.sig_done, base + s + 1)
                dense(pair(s), slot, src, range(CT), g.branch_done, off=s * P, width=2 * P)

            pe.wait_ge(glu_v, 3)
            with pe.Fori(0, 2) as i:
                for r in range(2):
                    u = U_ATT + 6 * i + 3 * r
                    base = 4 * i + 2 * r
                    for s in range(2):
                        gates(g_att, base, u + s, s, (r + s) % 2)
                    unit(u + 2)
                    for s in range(2):
                        branch(g_att, base, s, r % 2, rows(o_hi, o_lo))

            def m_query(h, p):
                half, k = p // 8, p % 8
                u = U_MQ + h
                if p == 0:
                    unit(u)
                if k == 0:
                    if h >= 1:
                        pe.wait_ge(mq_lo_done, 2 * h - 1 + half)
                    else:
                        pe.wait_ge(g_att.y_done, KT + 1)
                mm = step(bank(half), weight(u % 2, k * P), rows(h_hi, h_lo)(k, half), k == 0, k == KT - 1)
                if h < MH and k == KT - 1:
                    mm.then_inc(mq_done, 1)
                elif p == 15:
                    mm.then_inc(g_mem.gate_done, 1)

            def m_scores(n):
                h, i = n // 4, n % 4
                pe.wait_ge(mq_lo_done, 2 * h + i // 2 + 1)
                if n >= 2:
                    pe.wait_ge(at_m.exp_done, n - 1)
                for q in range(2):
                    a = slice((2 * i + q) * P, (2 * i + q + 1) * P)
                    mm = step(bank(4 + n % 2)[:, q * MEM:(q + 1) * MEM], (mq_hi[:, a], mq_lo[:, a]),
                              (mk_hi[:, h, :], mk_lo[:, h, :]), True, True)
                mm.then_inc(at_m.qk_done, 1)

            def m_turn(n):
                pe.wait_ge(at_m.norm_done, n + 1)
                if n >= 2:
                    pe.wait_ge(at_m.pt_lo_done, n - 1)
                for kt in range(MT):
                    for q in range(2):
                        a = kt * MEM + q * P
                        mm = nc.tensor.transpose(bank(6 + n % 2)[:, a:a + P], mp[:, n % 2, q, kt * P:(kt + 1) * P], ident[:])
                mm.then_inc(at_m.turned, 1)

            def m_values(n):
                h = n // 4
                pe.wait_ge(at_m.pt_lo_done, n + 1)
                if n >= 2:
                    pe.wait_ge(at_m.o_lo_done, n - 1)
                for kt in range(MT):
                    a, b = slice(h * P, (h + 1) * P), slice(kt * MEM, (kt + 1) * MEM)
                    mm = step(bank(2 + n % 2)[:, 0:MEM], (mv_hi[:, kt, a], mv_lo[:, kt, a]), (mpt_hi[:, b], mpt_lo[:, b]),
                              kt == 0, kt == MT - 1)
                mm.then_inc(at_m.pv_done, 1)

            for p in range(16):
                m_query(0, p)
            for n in range(16 + 1):
                h, i = n // 4, n % 4
                if n < 16:
                    m_scores(n)
                if n > 0:
                    m_turn(n - 1)
                for p in range(4 * i, 4 * i + 4) if n <= 12 else range(3 * n - 35, 3 * n - 32):
                    m_query(min(h, MH - 1) + 1, p)
                if n > 0:
                    m_values(n - 1)

            for dp in range(4):
                u = U_MEMO + 3 * dp
                for s in range(2):
                    if dp == 0 and s == 1:
                        pe.wait_ge(at_m.o_lo_done, 16)
                    if dp > 0 or s == 1:
                        gates(g_mem, 2 * dp, u + s, s, (u + s) % 2)
                    if dp == 3 and s == 0:
                        pe.wait_ge(ln_mean_in, CT - 1)
                        for half in range(2):
                            mm = nc.tensor.matmul(bank(4 + half), ones[:], ln_sum[:, half * HALF:(half + 1) * HALF],
                                                  start=True, stop=True)
                        mm.then_inc(ln_mean_done, 1)
                    if dp == 3 and s == 1:
                        norm_cols(n_ln, ln_sum, 0, T)
                unit(u + 2)
                for s in range(2):
                    branch(g_mem, 2 * dp, s, (u + 2) % 2, rows(o_hi, o_lo))
                    if dp == 3 and s == 0:
                        norm_spread(n_ln, ln_diag, 0, T)

            for dp in range(4):
                u = U_CONVO + 3 * dp
                for s in range(2):
                    if dp == 0:
                        pe.wait_ge(g_mem.mul_done, KT - 1 + s)
                    gates(g_conv, 2 * dp, u + s, s, (u + s) % 2)
                if dp == 0:
                    pe.wait_ge(*n_ln.past("lo_done", CT))
                unit(u + 2)
                for s in range(2):
                    branch(g_conv, 2 * dp, s, (u + 2) % 2, rows(c_hi, c_lo))

            unit(U_OUT)
            dense_two(U_OUT, (pair(2), pair(3)), rows(y_hi, y_lo), out_done, 1,
                      lambda half, k: pe.wait_ge(y_lo_done, k + 1))
            for d in range(2, KT - 2):
                slot = unit(U_OUT + d)
                if d >= 4:
                    pe.wait_ge(x_added, d - 3)
                dense(pair((d + 2) % 4), slot, rows(y_hi, y_lo), range(KT), out_done)
            for half in range(2):
                for d in (KT - 2, KT - 1):
                    slot = (U_OUT + d) % 2
                    if half == 0:
                        unit(U_OUT + d, first=(d == KT - 1))
                        pe.wait_ge(x_added, d - 3)
                    elif d == KT - 1:
                        release[0] = True
                    outs = [None, None]
                    outs[half] = pair((d + 2) % 4)[half]

                    def first_half_norm(k):
                        if (half, d, k) == (1, KT - 2, 5):
                            norm_cols(n_ffn2, acc, 0)
                        if (half, d, k) == (1, KT - 1, 1):
                            norm_spread(n_ffn2, diag, 0)

                    dense(outs, slot, rows(y_hi, y_lo), range(KT), out_done, hook=first_half_norm)

            ffn(f2, n_ffn2, n_fin, after_sums(n_ffn2, lambda half, k: None))
            norm_cols(n_fin, acc, 1)
            norm_spread(n_fin, diag, 1)

        @block.scalar
        def _(act):
            act.dma_start(params[:], params_in).then_inc(params_loaded, 16)
            load_x(act, 1)
            act.wait_ge(ext_zeroed, 1)
            act.dma_start(ext[:, FAR:FAR + REL], rel_in).then_inc(rel_loaded, 16)

            def copy(out, in_, done, scale=1.0):
                nc.scalar.activation(out, in_, ACT.Copy, scale=scale).then_inc(done, 1)

            def squares(n, i, src, buf, ready, bufs, width):
                h, k = n.order[i]
                ready(h, k)
                if i >= bufs:
                    act.wait_ge(*n.past("summed", n.sums(i - bufs)))
                nc.scalar.activation(buf[:, i % bufs, :], src[:, k, h * HALF:h * HALF + width],
                                     ACT.Square).then_inc(n.squared, 1)

            def x_squares(n, i, ready):
                squares(n, i, x, sq, ready, 4, HALF)

            def deviation(n, half=0, width=HALF, channels=D, b=None):
                act.wait_ge(*n.past("cols_done", half + 1))
                a, w = half * (HALF // P), width // P
                nc.scalar.activation(cols[:, 0, a:a + w], bank(4 + half if b is None else b)[:, 0:w], ACT.Sqrt,
                                     bias=eps[:], scale=1.0 / channels).then_inc(n.std_done, 1)

            def sqrt_table(column):
                nc.scalar.activation(spare[:, column:column + 1], eps[:], ACT.Sqrt)

            def round_tile(n, half, k):
                i = half * KT + k
                act.wait_ge(*n.past("scaled", i + 1))
                copy(h_hi[:, k, half * HALF:(half + 1) * HALF], nt[:, i % 4, :], n.hi_done)

            def norm_behind(n, ready, at_first=None, at_last=None):
                for i in range(2 * KT):
                    x_squares(n, i, ready)
                    if i == 0 and at_first is not None:
                        at_first()
                    if i == 2 * KT - 1 and at_last is not None:
                        at_last()
                    if i == FACTORS_AT:
                        deviation(n, 0)
                    for k in n.steps.get(i, ()):
                        round_tile(n, 0, k)
                deviation(n, 1)
                for k in range(6, KT):
                    round_tile(n, 0, k)
                for k in range(KT):
                    round_tile(n, 1, k)

            act.wait_ge(const_ready, 5)
            norm_behind(n_ffn1, lambda h, k: act.wait_ge(x_loaded[h][k // 2], 16))

            act.wait_ge(*n_ffn1.past("lo_done", 2 * KT))
            act.dma_start(mem[:], mem_in).then_inc(mem_loaded, 16)
            for k in range(KT):
                squares(n_mem, k, mem, msq, lambda h, k: act.wait_ge(mem_loaded, 16), 2, MEM)
            deviation(n_mem, 0, MEM, b=7)

            def round_memory_rows():
                for k in range(KT):
                    act.wait_ge(*n_mem.past("scaled", k + 1))
                    copy(mem_hi[:, k, :], mnt[:, k % 2, :], n_mem.hi_done)

            def bias_table():
                act.wait_ge(ext_ready, 1)
                act.dma_start(rel_ext.ap(), ext[:]).then_inc(ext_stored, 16)
                act.wait_ge(ext_stored, 16)
                act.dma_start(bias_rows,
                              bass.AP(rel_ext, P - 1, [[EXT, HEADS], [-1, P], [1, BANDK]])).then_inc(rows_stored, 16)

            def ffn(f):
                def tile(F, par, ff, first):
                    act.wait_ge(f.up_done, 2 * F + 1)
                    if not first:
                        act.wait_ge(f.prod_done, F - 1)
                    nc.scalar.activation(silu[:, ff, :], bank(4 * ff, 2), ACT.Silu).then_inc(f.silu_done, 1)

                def round_hidden(F, par, ff, used):
                    act.wait_ge(f.prod_done, F + 1)
                    if used is not None:
                        act.wait_ge(f.down_done, used)
                    copy(hid_hi[:, par, ff, :], prod[:, ff, :], f.hi_done)

                for ff in range(2):
                    tile(ff, 0, ff, True)
                    round_hidden(ff, 0, ff, None)
                    if f is f1 and ff == 0:
                        round_memory_rows()
                        bias_table()

                def turn(i, first):
                    for r in range(2):
                        for ff in range(2):
                            F = 4 * i + (2 + 2 * r + ff)
                            tile(F, 1 - r, ff, False)
                            round_hidden(F, 1 - r, ff, None if first and r == 0 else 16 * i + 8 * r)

                turn(0, True)
                with act.Fori(1, (PAIRS - 1) // 2) as i:
                    turn(i, False)

            ffn(f1)

            def x_ready(f):
                def ready(h, k):
                    act.wait_ge(f.acc_done, 8 * (PAIRS - 1) + h * KT + k + 1)
                return ready

            def move_memory():
                act.wait_ge(*n_mem.past("lo_done", KT))
                act.dma_start(mem_kept[0][:].bitcast(F32), mem_hi[:].bitcast(F32)).then_inc(mem_moved, 16)
                act.dma_start(mem_kept[1][:].bitcast(F32), mem_lo[:].bitcast(F32)).then_inc(mem_moved, 16)

            def spill():
                for k in range(KT):
                    act.dma_start(x_spill[k], x[:, k, :]).then_inc(x_spilled, 16)

            sqrt_table(0)
            norm_behind(n_mix, x_ready(f1), move_memory, spill)

            act.wait_ge(x_spilled, 16 * KT)
            act.wait_ge(*n_mix.past("lo_done", 2 * KT))
            act.wait_ge(rows_stored, 16)

            def load_bias(h):
                if h >= 2:
                    act.wait_ge(at_c.max_done, 8 * (h - 1))
                act.dma_start(bias[:, h % 2, :], bias_rows[h]).then_inc(bias_in[h % 2], 16)

            def round_half(t, c):
                which, half = c // 2, c % 2
                a, b = slice(half * HALF, (half + 1) * HALF), t % 2
                act.wait_ge(qkv_done, 6 * t + c + 1)
                if which == 2:
                    copy(vT[:, t, a], bank(half), vt_copied)
                else:
                    if t >= 2:
                        act.wait_ge(at_c.qk_done, 16 * (t - 1))
                    src = bank(half + (2 if t == 0 and which == 1 else 0))
                    copy((q_hi, k_hi)[which][b][:, a], src, qkv_hi, scale=(DH ** -0.5, 1.0)[which])

            def round_values(t, half):
                act.wait_ge(vt_turned, 2 * t + half + 1)
                if t >= 2:
                    act.wait_ge(at_c.pv_done, 8 * (t - 1))
                copy(v_hi[t % 2][:, 4 * half:4 * half + 4, :], bank(7).rearrange("p (c d) -> p c d", c=4), v_hi_done)

            def round_memory(c):
                act.wait_ge(kv_done, c + 1)
                if c < MH:
                    copy(mk_hi[:, c, :], bank(7)[:, 0:MEM], kv_hi)
                else:
                    copy(mv_hi[:, :, (c - MH) * 2 * P:(c - MH + 1) * 2 * P],
                         bank(7).rearrange("p (m d) -> p m d", m=MT), kv_hi)

            def copy_input(c):
                half = c % 2
                dst = (conv[:, 1, :], conv[:, 3, :], conv[:, 2, :], conv[:, 0, :])[c // 2]
                at_col = half * HALF + PAD
                act.wait_ge(ag_done, c + 1)
                if c == 0:
                    act.wait_ge(at_c.pv_done, 24)
                    act.wait_ge(vt_turned, 8)
                copy(dst[:, at_col:at_col + HALF], bank(half), ag_copied)

            def exps(n):
                w = item(n)[4]
                act.wait_ge(at_c.max_done, n + 1)
                nc.scalar.activation(pr[n % 2][:, 0:w], pr[n % 2][:, 0:w], ACT.Exp, bias=stat[:, 0, n % 2:n % 2 + 1],
                                     scale=-1.0, accum_out=stat[:, 1, n % 2:n % 2 + 1]).then_inc(at_c.exp_done, 1)

            def round_probs(n):
                w = item(n)[4]
                act.wait_ge(at_c.turned, n + 1)
                if n > 0 and n % 2 == 0:
                    act.wait_ge(at_c.pv_done, n // 2)
                copy(pt_hi[:, 0:w // P, 1 - n % 2, :], ps[:, turn_at:turn_at + w].rearrange("p (c k) -> p c k", k=P),
                     at_c.pt_hi_done)

            def round_out(n):
                t, b, e, j, w, key = item(n)
                act.wait_ge(at_c.pv_done, n // 2 + 1)
                r = slice(64 * e, 64 * e + 64)
                copy(o_hi[r, t, (j - 1) * P:(j + 1) * P], pair_out[r, :], at_c.o_hi_done)

            load_bias(0)
            load_bias(1)
            for c in range(6):
                round_half(0, c)
            round_values(0, 0)
            for n in range(N_ITEMS + 1):
                t, m = n // 16, n % 16
                if n > 0:
                    round_probs(n - 1)
                if n < N_ITEMS:
                    exps(n)
                if m == 15 and t < 3:
                    round_values(t + 1, 0)
                elif n in SECOND_TURNS:
                    round_values(t, 1)
                if n < N_ITEMS:
                    for kind, half in halves_done(n):
                        if t < 3:
                            round_half(t + 1, 2 * "qkv".index(kind) + half)
                        else:
                            copy_input(2 * ("a0", "g0", "a1", "g1").index(kind) + half)
                    for c in memory_done(n):
                        round_memory(c)
                if n > 0 and n % 2 == 0:
                    round_out(n - 1)
                if n % 8 == 7 and n // 8 + 2 < HEADS:
                    load_bias(n // 8 + 2)

            for t in range(CT):
                if t < 2:
                    act.wait_ge(ag_copied, 8)
                    g = conv[:, (3, 0)[t], PAD:PAD + T]
                    nc.scalar.activation(g, g, ACT.Sigmoid).then_inc(glu_sig, 1)
                else:
                    act.wait_ge(glu_done, 2 * (t - 2) + 2)
                    if t == 2:
                        act.wait_ge(at_c.pv_done, N_ITEMS // 2)
                    nc.scalar.activation(gate[:, t - 2, :], bank(4 * (t - 2) + 2, 2), ACT.Sigmoid).then_inc(glu_sig, 1)

            def sigmoids(g, base, s, col):
                act.wait_ge(g.gate_done, base + s + 1)
                act.wait_ge(g.y_done, base + s + 1)
                nc.scalar.activation(gate[:, s, :], bank(2 * s, 2), ACT.Sigmoid, bias=params[:, bass.ds(col, 1)]
                                     if not isinstance(col, int) else params[:, col:col + 1]).then_inc(g.sig_done, 1)

            act.wait_ge(glu_v, CT)
            with act.Fori(0, 4) as dp:
                for s in range(2):
                    sigmoids(g_att, 2 * dp, s, C_GATE + KT + 2 * dp + s)

            act.wait_ge(g_att.y_done, KT + 2)

            def m_query(h, halves):
                for half in halves:
                    act.wait_ge(mq_done, 2 * h + half + 1)
                    if h >= 1:
                        act.wait_ge(at_m.qk_done, 4 * h - 2 + 2 * half)
                    copy(mq_hi[:, half * HALF:(half + 1) * HALF], bank(half), mq_hi_done, scale=P ** -0.5)

            def m_exps(n):
                act.wait_ge(at_m.max_done, n + 1)
                if n >= 2:
                    act.wait_ge(at_m.turned, n - 1)
                for q in range(2):
                    c = 2 * (n % 2) + q
                    e = nc.scalar.activation(mp[:, n % 2, q, :], bank(4 + n % 2)[:, q * MEM:(q + 1) * MEM], ACT.Exp,
                                             bias=stat[:, 0, c:c + 1], accum_out=stat[:, 1, c:c + 1])
                e.then_inc(at_m.exp_done, 1)

            def m_round_probs(n):
                act.wait_ge(at_m.turned, n + 1)
                if n >= 1:
                    act.wait_ge(at_m.pv_done, n)
                copy(mpt_hi[:], bank(6 + n % 2), at_m.pt_hi_done)

            def m_round_out(n):
                act.wait_ge(at_m.pv_done, n + 1)
                copy(o_hi[:, n // 4, (n % 4) * MEM:(n % 4 + 1) * MEM], bank(2 + n % 2)[:, 0:MEM], at_m.o_hi_done)

            m_query(0, (0, 1))
            for n in range(16 + 1):
                if n > 0:
                    m_round_probs(n - 1)
                if n < 16:
                    m_exps(n)
                if n % 2 == 1 and n < 12:
                    m_query(n // 4 + 1, (n // 2 % 2,))
                if n > 0:
                    m_round_out(n - 1)

            def ln_squares():
                for c in range(CT):
                    squares(n_ln, c, conv[:, :, PAD:PAD + T], ln_sq, lambda h, c: act.wait_ge(ln_centred, c + 1), 2, T)

            for dp in range(4):
                for s in range(2):
                    sigmoids(g_mem, 2 * dp, s, C_GATE + 2 * KT + 2 * dp + s)
                    if dp == 3 and s == 0:
                        ln_squares()
            deviation(n_ln, 0, T, channels=CONV)

            def ln_out():
                for c in range(CT):
                    act.wait_ge(*n_ln.past("scaled", c + 1))
                    nc.scalar.activation(conv[:, c, PAD:PAD + T], conv[:, c, PAD:PAD + T], ACT.Silu,
                                         bias=params[:, C_LNB + c:C_LNB + c + 1]).then_inc(ln_silu_done, 1)
                    act.wait_ge(ln_silu_done, c + 1)
                    act.wait_ge(g_mem.branch_done, KT)
                    copy(c_hi[:, c, :], conv[:, c, PAD:PAD + T], n_ln.hi_done)

            ln_out()
            for dp in range(4):
                for s in range(2):
                    if dp == 0:
                        act.wait_ge(g_mem.y_done, KT + 1 + s)
                    sigmoids(g_conv, 2 * dp, s, C_GATE + 2 * dp + s)

            act.wait_ge(g_conv.gate_done, KT)
            for k in range(KT):
                act.wait_ge(g_conv.y_done, 2 + k + 1)
                copy(y_hi[:, k, :], y[:, k, :], y_hi_done)
            for k in range(KT):
                act.dma_start(x[:, k, :], x_spill[k]).then_inc(x_back[k], 16)

            def added(h, k):
                act.wait_ge(x_added, k + 1 if k < KT - 2 else KT - 2 + n_ffn2.order[-4:].index((h, k)) + 1)

            sqrt_table(1)
            for i in range(2 * KT - 2):
                x_squares(n_ffn2, i, added)
            deviation(n_ffn2, 0)
            x_squares(n_ffn2, 2 * KT - 2, added)
            for k in range(4):
                round_tile(n_ffn2, 0, k)
            x_squares(n_ffn2, 2 * KT - 1, added)
            for k in range(4, 6):
                round_tile(n_ffn2, 0, k)
            deviation(n_ffn2, 1)
            for k in range(6, KT):
                round_tile(n_ffn2, 0, k)
            for k in range(KT):
                round_tile(n_ffn2, 1, k)
            ffn(f2)
            sqrt_table(2)
            for i in range(2 * KT):
                x_squares(n_fin, i, x_ready(f2))
                if i == FACTORS_AT:
                    deviation(n_fin, 0)
            deviation(n_fin, 1)

        @block.vector
        def _(dve):
            dve.sem_inc(dw_done, 1)
            for g in (g_att, g_mem, g_conv):
                dve.sem_inc(g.y_done, 2)

            def cut(out, whole, hi, done):
                nc.vector.tensor_tensor(out, whole, hi.bitcast(F32), ALU.subtract).then_inc(done, 1)

            def add_squares(n, i, buf, bufs, a, width):
                h, k = n.order[i]
                if k == 0:
                    return
                dve.wait_ge(*n.past("squared", i + 1))
                to = a[:, h * HALF:h * HALF + width]
                if k == 1:
                    before = buf[:, n.order.index((h, 0)) % bufs, :]
                else:
                    before = to
                    dve.wait_ge(*n.past("summed", n.sums(n.order.index((h, k - 1)))))
                nc.vector.tensor_tensor(to, before, buf[:, i % bufs, :], ALU.add).then_inc(n.summed, 1)

            def x_sum(n, i):
                add_squares(n, i, sq, 4, acc, HALF)

            def factors(n, dg, half=0, width=HALF):
                w, a = width // P, half * (HALF // P)
                dve.wait_ge(*n.past("std_done", half + 1))
                nc.vector.reciprocal(cols[:, 1, a:a + w], cols[:, 0, a:a + w]).then_inc(n.rstd_done, 1)
                dve.wait_ge(*n.past("rstd_done", half + 1))
                for i in range(a, a + w):
                    d = nc.vector.tensor_scalar(dg[:, i * P:(i + 1) * P], ident[:], cols[:, 1, i:i + 1], None, ALU.mult)
                d.then_inc(n.diag_done, 1)

            def scale(n, out, src, gain, spread):
                nc.vector.scalar_tensor_tensor(out=out, in0=src, scalar=params[:, gain:gain + 1],
                                               in1=spread, op0=ALU.mult, op1=ALU.mult).then_inc(n.scaled, 1)

            def normalise(n, half, j, gain):
                a = slice(half * HALF, (half + 1) * HALF)
                if j == 0:
                    dve.wait_ge(*n.past("spread", half + 1))
                if j < KT:
                    i = half * KT + j
                    if i >= 4:
                        dve.wait_ge(*n.past("lo_done", i - 3))
                    scale(n, nt[:, i % 4, :], x[:, j, a], gain + j, bank(6 + half))
                if j >= 2:
                    i = half * KT + j - 2
                    dve.wait_ge(*n.past("hi_done", i + 1))
                    cut(h_lo[:, j - 2, a], nt[:, i % 4, :], h_hi[:, j - 2, a], n.lo_done)

            nc.vector.memset(ext[:], 0.0).then_inc(ext_zeroed, 1)
            nc.vector.memset(ext_zero[:], 0.0).then_inc(ext_zeroed, 1)
            def first_half(n, i, gain):
                if i == FACTORS_AT:
                    factors(n, diag, 0)
                for j in n.steps.get(i, ()):
                    normalise(n, 0, j, gain)

            def rest_of_norm(n, gain):
                for j in range(6, KT):
                    normalise(n, 0, j, gain)
                factors(n, diag, 1)
                for j in range(KT, KT + 2):
                    normalise(n, 0, j, gain)
                for j in range(KT + 2):
                    normalise(n, 1, j, gain)

            dve.wait_ge(ident_ready, 1)
            dve.wait_ge(params_loaded, 16)
            for i in range(2 * KT):
                x_sum(n_ffn1, i)
                first_half(n_ffn1, i, C_FFN1)
            rest_of_norm(n_ffn1, C_FFN1)

            dve.wait_ge(rel_loaded, 16)
            dve.wait_ge(ext_zeroed, 2)
            nc.vector.tensor_scalar(ext[:, 0:FAR], ext_zero[:], ext[:, FAR:FAR + 1], None,
                                    ALU.add).then_inc(ext_ready, 1)
            for k in range(KT):
                add_squares(n_mem, k, msq, 2, macc, MEM)
            factors(n_mem, mdiag, 0, MEM)
            def normalise_memory():
                dve.wait_ge(*n_mem.past("spread", 1))
                nc.vector.tensor_scalar(mspread[:], bank(7)[:, 0:MEM], 1.0, None, ALU.mult).then_inc(mem_spread_kept, 1)
                dve.wait_ge(mem_spread_kept, 1)
                for k in range(KT + 1):
                    if k < KT:
                        if k >= 2:
                            dve.wait_ge(*n_mem.past("lo_done", k - 1))
                        scale(n_mem, mnt[:, k % 2, :], mem[:, k, :], C_MEM + k, mspread[:])
                    if k >= 1:
                        dve.wait_ge(*n_mem.past("hi_done", k))
                        cut(mem_lo[:, k - 1, :], mnt[:, (k - 1) % 2, :], mem_hi[:, k - 1, :], n_mem.lo_done)

            def ffn(f, n_next, behind):
                def tile(F, par, ff, first):
                    dve.wait_ge(f.silu_done, F + 1)
                    dve.wait_ge(f.up_done, 2 * F + 2)
                    if not first:
                        dve.wait_ge(f.lo_done, F - 1)
                    nc.vector.tensor_tensor(prod[:, ff, :], silu[:, ff, :], bank(4 * ff + 2, 2), ALU.mult)\
                        .then_inc(f.prod_done, 1)
                    dve.wait_ge(f.hi_done, F + 1)
                    cut(hid_lo[:, par, ff, :], prod[:, ff, :], hid_hi[:, par, ff, :], f.lo_done)

                def add(down, before, d):
                    dve.wait_ge(f.down_done, down + (d + 1))
                    if before is not None:
                        dve.wait_ge(f.acc_done, before + (d + 1))
                    nc.vector.scalar_tensor_tensor(out=x[:, d, :], in0=bank(2 * (d % 4), 2), scalar=0.5, in1=x[:, d, :],
                                                   op0=ALU.mult, op1=ALU.add).then_inc(f.acc_done, 1)

                for ff in range(2):
                    tile(ff, 0, ff, True)
                    if f is f1 and ff == 0:
                        normalise_memory()

                def turn(i, first):
                    for r in range(2):
                        for ff in range(2):
                            tile(4 * i + (2 + 2 * r + ff), 1 - r, ff, False)
                        for d in range(KT):
                            add(16 * i + 8 * r, None if first and r == 0 else 16 * i + (8 * r - 8), d)

                if f is f1:
                    dve.wait_ge(ext_stored, 16)
                turn(0, True)
                with dve.Fori(1, (PAIRS - 1) // 2) as i:
                    turn(i, False)
                last = 8 * (PAIRS - 1)
                for n in range(2 * KT):
                    half, d = n // KT, n % KT
                    a = slice(half * HALF, (half + 1) * HALF)
                    dve.wait_ge(f.down_done, last + n + 1)
                    dve.wait_ge(f.acc_done, last - KT + d + 1)
                    nc.vector.scalar_tensor_tensor(out=x[:, d, a], in0=bank(d if half == 0 else d % 4), scalar=0.5,
                                                   in1=x[:, d, a], op0=ALU.mult, op1=ALU.add).then_inc(f.acc_done, 1)
                    if n >= 1:
                        x_sum(n_next, n - 1)
                    behind(n)
                x_sum(n_next, 2 * KT - 1)

            ffn(f1, n_mix, lambda n: first_half(n_mix, n, C_MIX))
            rest_of_norm(n_mix, C_MIX)

            def cut_half(t, c):
                which, half = c // 2, c % 2
                a, b = slice(half * HALF, (half + 1) * HALF), t % 2
                dve.wait_ge(qkv_hi, 4 * t + c + 1)
                nc.vector.scalar_tensor_tensor(out=(q_lo, k_lo)[which][b][:, a],
                                               in0=bank(half + (2 if t == 0 and which == 1 else 0)),
                                               scalar=(DH ** -0.5, 1.0)[which],
                                               in1=(q_hi, k_hi)[which][b][:, a].bitcast(F32), op0=ALU.mult,
                                               op1=ALU.subtract).then_inc(qkv_lo, 1)

            def cut_values(t, half):
                dve.wait_ge(v_hi_done, 2 * t + half + 1)
                a = slice(4 * half, 4 * half + 4)
                cut(v_lo[t % 2][:, a, :], bank(7).rearrange("p (c d) -> p c d", c=4), v_hi[t % 2][:, a, :], v_lo_done)

            def cut_memory(c):
                dve.wait_ge(kv_hi, c + 1)
                if c < MH:
                    cut(mk_lo[:, c, :], bank(7)[:, 0:MEM], mk_hi[:, c, :], kv_lo)
                else:
                    a = slice((c - MH) * 2 * P, (c - MH + 1) * 2 * P)
                    cut(mv_lo[:, :, a], bank(7).rearrange("p (m d) -> p m d", m=MT), mv_hi[:, :, a], kv_lo)

            def mask_bias(h):
                dve.wait_ge(bias_in[h % 2], 16 * (h // 2) + 16)
                nc.vector.memset(bias[0:64, h % 2, BANDK - 64:BANDK], NEG).then_inc(bias_masked, 1)
                nc.vector.memset(bias[64:P, h % 2, 0:64], NEG).then_inc(bias_masked, 1)
                dve.wait_ge(bias_masked, 2 * h + 2)

            def maxima(n):
                w = item(n)[4]
                dve.wait_ge(at_c.qk_done, n + 1)
                probs, scores = pr[n % 2][:, 0:w], bank(2, 2)[:, 0:w]
                biases = bias[:, n // 8 % 2, BANDK - w:BANDK]
                if w > HALF:
                    probs, biases = [v.rearrange("p (c k) -> p c k", c=2) for v in (probs, biases)]
                    scores = bank(2, 2).rearrange("p (c k) -> p c k", c=2)[:, :, 0:w // 2]
                nc.vector.tensor_tensor_reduce(probs, scores, biases, -1.0, BIG,
                                               ALU.add, ALU.min, stat[:, 0, n % 2:n % 2 + 1]).then_inc(at_c.max_done, 1)

            def normalise_probs(n):
                w, c = item(n)[4], slice(n % 2, n % 2 + 1)
                dve.wait_ge(at_c.exp_done, n + 1)
                nc.vector.reciprocal(stat[:, 2, c], stat[:, 1, c]).then_inc(at_c.rcp_done, 1)
                dve.wait_ge(at_c.rcp_done, n + 1)
                nc.vector.tensor_scalar(pr[n % 2][:, 0:w], pr[n % 2][:, 0:w], stat[:, 2, c], None,
                                        ALU.mult).then_inc(at_c.norm_done, 1)

            def cut_probs(n):
                w = item(n)[4]
                dve.wait_ge(at_c.pt_hi_done, n + 1)
                a = slice(0, w // P), 1 - n % 2
                cut(pt_lo[:, a[0], a[1], :], ps[:, turn_at:turn_at + w].rearrange("p (c k) -> p c k", k=P),
                    pt_hi[:, a[0], a[1], :], at_c.pt_lo_done)

            def cut_out(n):
                t, b, e, j, w, key = item(n)
                dve.wait_ge(at_c.o_hi_done, n // 2 + 1)
                r, a = slice(64 * e, 64 * e + 64), slice((j - 1) * P, (j + 1) * P)
                cut(o_lo[r, t, a], pair_out[r, :], o_hi[r, t, a], at_c.o_lo_done)

            for c in range(4):
                cut_half(0, c)
            cut_values(0, 0)
            for n in range(N_ITEMS + 1):
                t, m = n // 16, n % 16
                if n < N_ITEMS:
                    if n % 8 == 0:
                        mask_bias(n // 8)
                    maxima(n)
                if n > 0:
                    cut_probs(n - 1)
                if n < N_ITEMS:
                    normalise_probs(n)
                if m == 15 and t < 3:
                    cut_values(t + 1, 0)
                elif n in SECOND_TURNS:
                    cut_values(t, 1)
                if n < N_ITEMS and t < 3:
                    for kind, half in halves_done(n):
                        if kind != "v":
                            cut_half(t + 1, 2 * "qk".index(kind) + half)
                    for c in memory_done(n):
                        cut_memory(c)
                if n > 0 and n % 2 == 0:
                    cut_out(n - 1)

            dve.wait_ge(ag_copied, 1)
            nc.vector.memset(conv[:, 1:5, 0:PAD], 0.0).then_inc(pad_done, 1)
            for t in range(CT):
                dve.wait_ge(glu_sig, t + 1)
                v = conv[:, t + 1, PAD:PAD + T]
                if t < 2:
                    a, g = v, conv[:, (3, 0)[t], PAD:PAD + T]
                else:
                    a, g = bank(4 * (t - 2), 2), gate[:, t - 2, :]
                if t == 2:
                    dve.wait_ge(glu_v, 1)
                nc.vector.tensor_tensor(v, g, a, ALU.mult).then_inc(glu_v, 1)

            def taps(c, lo, hi):
                for tap in range(lo, hi):
                    src = conv[:, c + 1, tap:tap + T]
                    dst = conv[:, c, PAD:PAD + T]
                    w = params[:, bass.ds(C_DW + TAPS * c + tap, 1)]
                    dve.wait_ge(dw_done, TAPS * c + (tap + 1))
                    if tap == 0:
                        nc.vector.tensor_scalar(dst, src, w, params[:, bass.ds(C_DWB + c, 1)], ALU.mult,
                                                ALU.add).then_inc(dw_done, 1)
                    else:
                        nc.vector.scalar_tensor_tensor(out=dst, in0=src, scalar=w, in1=dst, op0=ALU.mult,
                                                       op1=ALU.add).then_inc(dw_done, 1)

            def mix(g, base, d, s, first):
                dve.wait_ge(g.branch_done, base + s + 1)
                dve.wait_ge(g.sig_done, base + s + 1)
                if first:
                    nc.vector.tensor_tensor(y[:, d, :], gate[:, s, :], bank(2 * s, 2), ALU.mult).then_inc(g.y_done, 1)
                else:
                    nc.vector.tensor_tensor(gate[:, s, :], gate[:, s, :], bank(2 * s, 2), ALU.mult).then_inc(g.mul_done, 1)
                    dve.wait_ge(g.mul_done, base + s + 1)
                    nc.vector.tensor_tensor(y[:, d, :], y[:, d, :], gate[:, s, :], ALU.add).then_inc(g.y_done, 1)

            dve.wait_ge(pad_done, 1)
            dve.wait_ge(glu_v, CT)
            cut_at = (0, 12, 16, 28, TAPS)

            with dve.Fori(0, 2) as i:
                for r in range(2):
                    taps(i, cut_at[2 * r], cut_at[2 * r + 1])
                    mix(g_att, 4 * i + 2 * r, 4 * i + 2 * r, 0, True)
                    taps(i, cut_at[2 * r + 1], cut_at[2 * r + 2])
                    mix(g_att, 4 * i + 2 * r, 4 * i + (2 * r + 1), 1, True)

            def m_query(h, halves):
                for half in halves:
                    dve.wait_ge(mq_hi_done, 2 * h + half + 1)
                    a = slice(half * HALF, (half + 1) * HALF)
                    nc.vector.scalar_tensor_tensor(out=mq_lo[:, a], in0=bank(half), scalar=P ** -0.5,
                                                   in1=mq_hi[:, a].bitcast(F32), op0=ALU.mult,
                                                   op1=ALU.subtract).then_inc(mq_lo_done, 1)

            def m_max(n):
                c = 2 * (n % 2)
                dve.wait_ge(at_m.qk_done, n + 1)
                nc.vector.tensor_reduce(stat[:, 0, c:c + 2], bank(4 + n % 2).rearrange("p (q k) -> p q k", q=2), AX.X,
                                        ALU.max, negate=True).then_inc(at_m.max_done, 1)

            def m_normalise(n):
                c = 2 * (n % 2)
                dve.wait_ge(at_m.exp_done, n + 1)
                nc.vector.reciprocal(stat[:, 2, c:c + 2], stat[:, 1, c:c + 2]).then_inc(at_m.rcp_done, 1)
                dve.wait_ge(at_m.rcp_done, n + 1)
                for q in range(2):
                    last = nc.vector.tensor_scalar(mp[:, n % 2, q, :], mp[:, n % 2, q, :], stat[:, 2, c + q:c + q + 1],
                                                   None, ALU.mult)
                last.then_inc(at_m.norm_done, 1)

            def m_cut_probs(n):
                dve.wait_ge(at_m.pt_hi_done, n + 1)
                cut(mpt_lo[:], bank(6 + n % 2), mpt_hi[:], at_m.pt_lo_done)

            def m_cut_out(n):
                dve.wait_ge(at_m.o_hi_done, n + 1)
                a = slice((n % 4) * MEM, (n % 4 + 1) * MEM)
                cut(o_lo[:, n // 4, a], bank(2 + n % 2)[:, 0:MEM], o_hi[:, n // 4, a], at_m.o_lo_done)

            m_query(0, (0, 1))
            for n in range(16 + 1):
                if n > 0:
                    m_cut_probs(n - 1)
                if n < 16:
                    m_max(n)
                    m_normalise(n)
                if n % 2 == 1 and n < 12:
                    m_query(n // 4 + 1, (n // 2 % 2,))
                if n > 0:
                    m_cut_out(n - 1)

            def taps_between(lo, hi):
                for n in range(lo, hi):
                    taps(2 + n // TAPS, n % TAPS, n % TAPS + 1)

            for dp in range(3):
                taps_between(21 * dp, min(21 * dp + 16, 2 * TAPS))
                mix(g_mem, 2 * dp, 2 * dp, 0, False)
                taps_between(min(21 * dp + 16, 2 * TAPS), min(21 * dp + 21, 2 * TAPS))
                mix(g_mem, 2 * dp, 2 * dp + 1, 1, False)

            dve.wait_ge(dw_done, CT * TAPS + 1)
            for c in range(1, CT):
                if c >= 2:
                    dve.wait_ge(ln_mean_in, c - 1)
                nc.vector.tensor_tensor(ln_sum, conv[:, 0, PAD:PAD + T] if c == 1 else ln_sum, conv[:, c, PAD:PAD + T],
                                        ALU.add).then_inc(ln_mean_in, 1)
            dve.wait_ge(ln_mean_done, 1)
            for c in range(CT):
                nc.vector.scalar_tensor_tensor(out=conv[:, c, PAD:PAD + T], in0=bank(4, 2), scalar=-1.0 / CONV,
                                               in1=conv[:, c, PAD:PAD + T], op0=ALU.mult, op1=ALU.add).then_inc(ln_centred, 1)
            for c in range(CT):
                add_squares(n_ln, c, ln_sq, 2, ln_sum, T)
            factors(n_ln, ln_diag, 0, T)
            mix(g_mem, 6, 6, 0, False)
            dve.wait_ge(*n_ln.past("spread", 1))
            dve.wait_ge(ln_centred, CT)
            for c in range(CT):
                scale(n_ln, conv[:, c, PAD:PAD + T], conv[:, c, PAD:PAD + T], C_LNG + c, bank(6, 2))
            mix(g_mem, 6, 7, 1, False)
            for c in range(CT):
                dve.wait_ge(*n_ln.past("hi_done", c + 1))
                cut(c_lo[:, c, :], conv[:, c, PAD:PAD + T], c_hi[:, c, :], n_ln.lo_done)

            def cut_y(k):
                dve.wait_ge(y_hi_done, k + 1)
                cut(y_lo[:, k, :], y[:, k, :], y_hi[:, k, :], y_lo_done)

            for d in range(KT - 2):
                mix(g_conv, d - d % 2, d, d % 2, False)
            for k in range(4):
                cut_y(k)
            mix(g_conv, 6, 6, 0, False)
            for k in range(4, 6):
                cut_y(k)
            mix(g_conv, 6, 7, 1, False)
            for k in range(6, 8):
                cut_y(k)

            def add_mixture(done, d, half=None):
                a = slice(0, T) if half is None else slice(half * HALF, (half + 1) * HALF)
                dve.wait_ge(out_done, done)
                dve.wait_ge(x_back[d], 16)
                src = bank(2 * ((d + 2) % 4), 2) if half is None else bank(2 * ((d + 2) % 4) + half)
                nc.vector.tensor_tensor(x[:, d, a], x[:, d, a], src, ALU.add).then_inc(x_added, 1)

            for d in range(KT - 2):
                add_mixture(d + 1, d)
                if d >= 1:
                    x_sum(n_ffn2, 2 * d - 2)
                    x_sum(n_ffn2, 2 * d - 1)
            add_mixture(KT - 1, KT - 2, 0)
            x_sum(n_ffn2, 2 * KT - 6)
            x_sum(n_ffn2, 2 * KT - 5)
            add_mixture(KT, KT - 1, 0)
            x_sum(n_ffn2, 2 * KT - 4)
            x_sum(n_ffn2, 2 * KT - 3)
            factors(n_ffn2, diag, 0)
            add_mixture(KT + 1, KT - 2, 1)
            for j in range(6):
                normalise(n_ffn2, 0, j, C_FFN2)
            add_mixture(KT + 2, KT - 1, 1)
            x_sum(n_ffn2, 2 * KT - 2)
            x_sum(n_ffn2, 2 * KT - 1)
            rest_of_norm(n_ffn2, C_FFN2)

            def scale_out(half, k):
                a = slice(half * HALF, (half + 1) * HALF)
                if k == 0:
                    dve.wait_ge(*n_fin.past("spread", half + 1))
                scale(n_fin, x[:, k, a], x[:, k, a], C_FINAL + k, bank(6 + half))

            def final_norm(n):
                if n == KT + 3:
                    scale_out(0, 0)
                if n == FACTORS_AT:
                    factors(n_fin, diag, 0)

            ffn(f2, n_fin, final_norm)
            for k in range(1, 3):
                scale_out(0, k)
            factors(n_fin, diag, 1)
            for k in range(3, KT):
                scale_out(0, k)
            for k in range(KT):
                scale_out(1, k)


def stream(inputs):
    import numpy as np

    def cut(w, rows, width):
        w = np.asarray(w)
        r, c = w.shape
        b = w.reshape(r // rows, rows // P, P, c // width, width)
        return b.transpose(0, 3, 2, 1, 4).reshape(r // rows, c // width, P, rows // P * width)

    units = []

    def ffn(up, down):
        up, down = cut(up[0], D, P)[0], cut(down[0], 2 * P, 4 * P)
        tiles = D_FF // P
        for g in range(PAIRS + 1):
            if g < PAIRS:
                for f in (2 * g, 2 * g + 1):
                    units.extend([up[f], up[tiles + f]])
            if g > 0:
                units.extend(down[g - 1])

    w_in = cut(inputs["w_in"][0], D, P)[0]
    a0, m0, g0 = 2 * CT, 2 * CT + 12, 2 * CT + 16

    def branch(b, w):
        w = cut(w[0], CONV, 2 * P)[0]
        for dp in range(KT // 2):
            units.extend([w_in[g0 + KT * b + 2 * dp], w_in[g0 + KT * b + 2 * dp + 1], w[dp]])

    ffn(inputs["ffn1_w_up"], inputs["ffn1_w_down"])
    keys, values = np.split(inputs["mem_w_kv"][0], 2, axis=1)
    kv = [*cut(keys, D, P)[0], *cut(values, 4 * P, 2 * P).transpose(1, 0, 2, 3).reshape(4, P, T)]
    for t in range(4):
        units.append(w_in[a0 + t])
        if t in (1, 2):
            units.extend(kv[4 * t - 4:4 * t - 2])
        units.append(w_in[a0 + 4 + t])
        if t in (1, 2):
            units.extend(kv[4 * t - 2:4 * t])
        units.append(w_in[a0 + 8 + t])
    for t in range(CT):
        units.extend([w_in[t], w_in[CT + t]])
    branch(1, inputs["att_w_o"])
    units.extend(w_in[m0:m0 + MH])
    branch(2, inputs["mem_w_o"])
    branch(0, inputs["conv_w_pw"])
    units.extend(cut(inputs["w_out"][0], D, P)[0])
    ffn(inputs["ffn2_w_up"], inputs["ffn2_w_down"])
    assert len(units) == UNITS
    return np.stack(units)


def kernel(**inputs):
    import numpy as np
    import concourse.bacc as bacc
    from concourse.bass_utils import run_bass_kernel_spmd

    inputs = {k: np.asarray(v) for k, v in inputs.items()}

    def columns(v):
        return v.reshape(-1, P).T

    params = np.concatenate(
        [columns(inputs[n].reshape(-1)) for n in ("ffn1_norm", "mix_norm", "mem_norm", "ffn2_norm", "final_norm", "b_gate")]
        + [inputs["conv_dw_w"][0].reshape(TAPS, CT, P).transpose(2, 1, 0).reshape(P, CT * TAPS)]
        + [columns(inputs[n][0]) for n in ("conv_dw_b", "conv_ln_g", "conv_ln_b")], axis=1)
    arrays = {
        "x_in": np.ascontiguousarray(inputs["x"][0].T).reshape(KT, P, T),
        "mem_in": np.ascontiguousarray(inputs["mem"][0].reshape(MEM, KT, P).transpose(2, 1, 0)),
        "weights": stream(inputs),
        "params": np.ascontiguousarray(params),
        "rel_bias": np.ascontiguousarray(inputs["att_rel_bias"][0][:, ::-1]),
    }
    nc = bacc.Bacc("TRN2", target_bir_lowering=False, num_devices=1)
    args = [nc.dram_tensor(n, a.shape, F32, kind="ExternalInput").ap() for n, a in arrays.items()]
    out = nc.dram_tensor("y_out", (KT, P, T), F32, kind="ExternalOutput").ap()
    program(nc, *args, out)
    r = run_bass_kernel_spmd(nc, [arrays], core_ids=[0])
    return np.ascontiguousarray(r.results[0]["y_out"].reshape(D, T).T)[None]
```
